# Optimizing a Trainium2 kernel written in Bass

```python
import jax, jax.numpy as jnp
from jax import lax
import numpy as np

D_MODEL = 1024
BATCH = 1
SEQ = 512
DEPTH = 1

HEAD_DIM = D_MODEL // 16
ATTN_HEADS = 6
ATTN_WIDTH = ATTN_HEADS * HEAD_DIM
ATTN_PATTERNS = ((128, 1), (512, 4), (2048, 16))
HEADS_PER_PATTERN = ATTN_HEADS // len(ATTN_PATTERNS)
CONV_GROUPS = 4
CONV_WIDTH = CONV_GROUPS * HEAD_DIM
CONV_TAPS = 31
LRU_HEADS = 6
LRU_WIDTH = LRU_HEADS * HEAD_DIM
LRU_CONV_TAPS = 4
LRU_C = 8.0
MIX_WIDTH = ATTN_WIDTH + CONV_WIDTH + LRU_WIDTH
D_FF = 4 * D_MODEL
RMS_EPS = 1e-6
LN_EPS = 1e-5

Q0 = 0
K0 = Q0 + ATTN_WIDTH
V0 = K0 + ATTN_WIDTH
CA0 = V0 + ATTN_WIDTH
CG0 = CA0 + CONV_WIDTH
LG0 = CG0 + CONV_WIDTH
LX0 = LG0 + LRU_WIDTH
IN_COLS = LX0 + LRU_WIDTH


def rmsnorm(x, g):
    xf = x.astype(jnp.float32)
    y = xf * lax.rsqrt(jnp.mean(xf * xf, axis=-1, keepdims=True) + RMS_EPS)
    return y.astype(x.dtype) * g

def layernorm(x, g, b):
    xf = x.astype(jnp.float32)
    mu = jnp.mean(xf, axis=-1, keepdims=True)
    var = jnp.mean(jnp.square(xf - mu), axis=-1, keepdims=True)
    y = (xf - mu) * lax.rsqrt(var + LN_EPS)
    return y.astype(x.dtype) * g + b

def alibi_slopes(n):
    return jnp.asarray(2.0 ** (-8.0 * np.arange(1, n + 1) / n), dtype=jnp.float32)

def causal_depthwise_conv(x, w, b):
    K, C = w.shape
    y = lax.conv_general_dilated(x, w[:, None, :], window_strides=(1,), padding=[(K - 1, 0)],
                                 dimension_numbers=("NWC", "WIO", "NWC"), feature_group_count=C)
    return y + b

def dilated_window_attention(q, k, v, slopes, window, dilation):
    B, S, H, Dh = q.shape
    W = window // dilation
    L = S // dilation
    nb = -(-L // W)
    Lp = nb * W

    def to_blocks(t):
        t = t.reshape(B, L, dilation, H, Dh).transpose(0, 2, 3, 1, 4)
        t = jnp.pad(t, ((0, 0), (0, 0), (0, 0), (0, Lp - L), (0, 0)))
        return t.reshape(B, dilation, H, nb, W, Dh)

    def with_prev(t):
        prev = jnp.pad(t, ((0, 0), (0, 0), (0, 0), (1, 0), (0, 0), (0, 0)))[:, :, :, :-1]
        return jnp.concatenate([prev, t], axis=4)

    qb = to_blocks(q)
    kb = with_prev(to_blocks(k))
    vb = with_prev(to_blocks(v))
    s = jnp.einsum("brhnqc,brhnkc->brhnqk", qb, kb).astype(jnp.float32) * (Dh ** -0.5)
    qi = jnp.arange(W)[:, None]
    kj = jnp.arange(2 * W)[None, :]
    dist = qi + W - kj
    band = (dist >= 0) & (dist <= W)
    has_prev = (jnp.arange(nb)[:, None, None] > 0) | (kj[None] >= W)
    valid = band[None] & has_prev
    bias = -slopes[:, None, None] * (dilation * dist).astype(jnp.float32)[None]
    s = jnp.where(valid[None, None, None], s + bias[None, None, :, None], -jnp.inf)
    m = jnp.max(s, axis=-1, keepdims=True)
    p = jnp.exp(s - m)
    l = jnp.sum(p, axis=-1, keepdims=True)
    o = jnp.einsum("brhnqk,brhnkc->brhnqc", p, vb.astype(jnp.float32)) / l
    lse = (m + jnp.log(l))[..., 0]
    o = o.reshape(B, dilation, H, Lp, Dh)[:, :, :, :L].transpose(0, 3, 1, 2, 4).reshape(B, S, H, Dh)
    lse = lse.reshape(B, dilation, H, Lp)[..., :L].transpose(0, 3, 1, 2).reshape(B, S, H)
    return o, lse

def attention_mixer(q, k, v):
    B, S = q.shape[:2]
    slopes = alibi_slopes(ATTN_HEADS)
    outs, lses = [], []
    for g, (window, dilation) in enumerate(ATTN_PATTERNS):
        sl = slice(g * HEADS_PER_PATTERN, (g + 1) * HEADS_PER_PATTERN)
        o, lse = dilated_window_attention(q[:, :, sl], k[:, :, sl], v[:, :, sl], slopes[sl], window, dilation)
        outs.append(o)
        lses.append(lse)
    o = jnp.stack(outs, axis=2)
    lse = jnp.stack(lses, axis=2)
    alpha = jax.nn.softmax(lse, axis=2)
    return (o * alpha[..., None]).reshape(B, S, ATTN_WIDTH).astype(q.dtype)

def conv_module(a, gate, dw_w, dw_b, ln_g, ln_b):
    u = a * jax.nn.sigmoid(gate)
    u = causal_depthwise_conv(u, dw_w, dw_b)
    u = layernorm(u, ln_g, ln_b)
    return jax.nn.silu(u)

def rg_lru(x, w_a, b_a, w_x, b_x, lam):
    B, S, C = x.shape
    xh = x.reshape(B, S, LRU_HEADS, C // LRU_HEADS)
    r = jax.nn.sigmoid(jnp.einsum("bshi,hio->bsho", xh, w_a).reshape(B, S, C) + b_a)
    i = jax.nn.sigmoid(jnp.einsum("bshi,hio->bsho", xh, w_x).reshape(B, S, C) + b_x)
    log_a = -LRU_C * r.astype(jnp.float32) * jax.nn.softplus(-lam.astype(jnp.float32))
    a = jnp.exp(log_a)
    b = jnp.sqrt(-jnp.expm1(2.0 * log_a)) * (i * x).astype(jnp.float32)

    def combine(left, right):
        a1, b1 = left
        a2, b2 = right
        return a1 * a2, a2 * b1 + b2

    _, h = lax.associative_scan(combine, (a, b), axis=1)
    return h.astype(x.dtype)

def recurrent_mixer(gate, xr, cw, cb, w_a, b_a, w_x, b_x, lam):
    u = causal_depthwise_conv(xr, cw, cb)
    return jax.nn.gelu(gate) * rg_lru(u, w_a, b_a, w_x, b_x, lam)

def hybrid_layer(x, norm1_g, w_in, conv_dw_w, conv_dw_b, conv_ln_g, conv_ln_b,
                 lru_conv_w, lru_conv_b, lru_wa, lru_ba, lru_wx, lru_bx, lru_lambda,
                 w_out, norm2_g, w_up, w_down):
    B, S, _ = x.shape
    h = rmsnorm(x, norm1_g)
    z = jnp.einsum("bsd,dc->bsc", h, w_in)
    q = z[..., Q0:K0].reshape(B, S, ATTN_HEADS, HEAD_DIM)
    k = z[..., K0:V0].reshape(B, S, ATTN_HEADS, HEAD_DIM)
    v = z[..., V0:CA0].reshape(B, S, ATTN_HEADS, HEAD_DIM)
    y_attn = attention_mixer(q, k, v)
    y_conv = conv_module(z[..., CA0:CG0], z[..., CG0:LG0], conv_dw_w, conv_dw_b, conv_ln_g, conv_ln_b)
    y_lru = recurrent_mixer(z[..., LG0:LX0], z[..., LX0:IN_COLS], lru_conv_w, lru_conv_b,
                            lru_wa, lru_ba, lru_wx, lru_bx, lru_lambda)
    mix = jnp.concatenate([y_attn, y_conv, y_lru], axis=-1)
    x = x + jnp.einsum("bsc,cd->bsd", mix, w_out)
    h2 = rmsnorm(x, norm2_g)
    ff = jnp.square(jax.nn.relu(jnp.einsum("bsd,df->bsf", h2, w_up)))
    return x + jnp.einsum("bsf,fd->bsd", ff, w_down)

def first_inputs(seed: int = 0) -> dict:
    key = jax.random.key(seed)
    ks = jax.random.split(key, 20)
    n = jax.random.normal
    f32 = jnp.float32
    x = n(ks[0], (BATCH, SEQ, D_MODEL), f32)
    norm1_g = 1.0 + 0.02 * n(ks[1], (DEPTH, D_MODEL), f32)
    w_in = n(ks[2], (DEPTH, D_MODEL, IN_COLS), f32) * D_MODEL ** -0.5
    conv_dw_w = n(ks[3], (DEPTH, CONV_TAPS, CONV_WIDTH), f32) * CONV_TAPS ** -0.5
    conv_dw_b = 0.02 * n(ks[4], (DEPTH, CONV_WIDTH), f32)
    conv_ln_g = 1.0 + 0.02 * n(ks[5], (DEPTH, CONV_WIDTH), f32)
    conv_ln_b = 0.02 * n(ks[6], (DEPTH, CONV_WIDTH), f32)
    lru_conv_w = n(ks[7], (DEPTH, LRU_CONV_TAPS, LRU_WIDTH), f32) * LRU_CONV_TAPS ** -0.5
    lru_conv_b = 0.02 * n(ks[8], (DEPTH, LRU_WIDTH), f32)
    blk = LRU_WIDTH // LRU_HEADS
    lru_wa = n(ks[9], (DEPTH, LRU_HEADS, blk, blk), f32) * blk ** -0.5
    lru_ba = 0.02 * n(ks[10], (DEPTH, LRU_WIDTH), f32)
    lru_wx = n(ks[11], (DEPTH, LRU_HEADS, blk, blk), f32) * blk ** -0.5
    lru_bx = 0.02 * n(ks[12], (DEPTH, LRU_WIDTH), f32)
    a_c = jax.random.uniform(ks[13], (DEPTH, LRU_WIDTH), f32, 0.9, 0.999)
    a0 = a_c ** (1.0 / LRU_C)
    lru_lambda = jnp.log(a0) - jnp.log1p(-a0)
    w_out = n(ks[14], (DEPTH, MIX_WIDTH, D_MODEL), f32) * MIX_WIDTH ** -0.5
    norm2_g = 1.0 + 0.02 * n(ks[15], (DEPTH, D_MODEL), f32)
    w_up = n(ks[16], (DEPTH, D_MODEL, D_FF), f32) * D_MODEL ** -0.5
    w_down = n(ks[17], (DEPTH, D_FF, D_MODEL), f32) * D_FF ** -0.5
    final_g = 1.0 + 0.02 * n(ks[18], (D_MODEL,), f32)
    return {"x": x, "norm1_g": norm1_g, "w_in": w_in, "conv_dw_w": conv_dw_w, "conv_dw_b": conv_dw_b,
            "conv_ln_g": conv_ln_g, "conv_ln_b": conv_ln_b, "lru_conv_w": lru_conv_w, "lru_conv_b": lru_conv_b,
            "lru_wa": lru_wa, "lru_ba": lru_ba, "lru_wx": lru_wx, "lru_bx": lru_bx, "lru_lambda": lru_lambda,
            "w_out": w_out, "norm2_g": norm2_g, "w_up": w_up, "w_down": w_down, "final_g": final_g}

def first_block(x, norm1_g, w_in, conv_dw_w, conv_dw_b, conv_ln_g, conv_ln_b, lru_conv_w, lru_conv_b,
              lru_wa, lru_ba, lru_wx, lru_bx, lru_lambda, w_out, norm2_g, w_up, w_down, final_g):
    for l in range(DEPTH):
        x = hybrid_layer(x, norm1_g[l], w_in[l], conv_dw_w[l], conv_dw_b[l], conv_ln_g[l], conv_ln_b[l],
                         lru_conv_w[l], lru_conv_b[l], lru_wa[l], lru_ba[l], lru_wx[l], lru_bx[l], lru_lambda[l],
                         w_out[l], norm2_g[l], w_up[l], w_down[l])
    return rmsnorm(x, final_g)


DEPTH_2 = 2

MLA_HEADS = 8
QK_NOPE_DIM = 64
QK_ROPE_DIM = 32
V_HEAD_DIM = 64
Q_LORA_RANK = 256
KV_LORA_RANK = 128
QK_HEAD_DIM = QK_NOPE_DIM + QK_ROPE_DIM
D_ATTN = MLA_HEADS * V_HEAD_DIM
ROPE_THETA = 10000.0
Q_BLOCK = 128
SSD_HEADS = 8
SSD_HEAD_DIM = 64
SSD_GROUPS = 2
SSD_STATE = 128
CONV_WIDTH_2 = 4
CHUNK = 128
D_SSD = SSD_HEADS * SSD_HEAD_DIM
D_CONV = D_SSD + 2 * SSD_GROUPS * SSD_STATE
D_MIX = D_ATTN + D_SSD
D_IN = Q_LORA_RANK + KV_LORA_RANK + QK_ROPE_DIM + D_SSD + D_CONV + SSD_HEADS
D_FF_2 = ((-(-8 * D_MODEL // 3) + 255) // 256) * 256
N_MOD = 6
EPS = 1e-6


def rmsnorm_2(x, w):
    xf = x.astype(jnp.float32)
    y = xf * lax.rsqrt(jnp.mean(xf * xf, axis=-1, keepdims=True) + EPS)
    return (y * w.astype(jnp.float32)).astype(x.dtype)

def rope(x, cos, sin):
    x1, x2 = jnp.split(x, 2, axis=-1)
    return jnp.concatenate([x1 * cos - x2 * sin, x2 * cos + x1 * sin], axis=-1)

def causal_attention(q, k, v):
    b, h, s, d = q.shape
    nb = s // Q_BLOCK
    scale = d ** -0.5
    qb = q.reshape(b, h, nb, Q_BLOCK, d).transpose(2, 0, 1, 3, 4)
    kpos = jnp.arange(s)

    def one_block(args):
        qi, i = args
        sc = jnp.einsum('bhqd,bhkd->bhqk', qi, k).astype(jnp.float32) * scale
        qpos = i * Q_BLOCK + jnp.arange(Q_BLOCK)
        mask = kpos[None, :] <= qpos[:, None]
        sc = jnp.where(mask, sc, jnp.finfo(jnp.float32).min)
        p = jax.nn.softmax(sc, axis=-1)
        return jnp.einsum('bhqk,bhkd->bhqd', p.astype(v.dtype), v)

    out = lax.map(one_block, (qb, jnp.arange(nb)))
    return out.transpose(1, 0, 3, 2, 4).reshape(b, s, h * v.shape[-1])

def ssd_chunked(x, dt, a, bm, cm):
    b, l, h, p = x.shape
    rep = h // bm.shape[2]
    nc = l // CHUNK
    xf = x.astype(jnp.float32)
    xdt = xf * dt[..., None]
    adt = dt * a
    bh = jnp.repeat(bm.astype(jnp.float32), rep, axis=2)
    ch = jnp.repeat(cm.astype(jnp.float32), rep, axis=2)
    n = bh.shape[-1]
    xc = xdt.reshape(b, nc, CHUNK, h, p)
    bc = bh.reshape(b, nc, CHUNK, h, n)
    cc = ch.reshape(b, nc, CHUNK, h, n)
    acs = jnp.cumsum(adt.reshape(b, nc, CHUNK, h), axis=2)
    seg = acs[:, :, :, None, :] - acs[:, :, None, :, :]
    tri = jnp.tril(jnp.ones((CHUNK, CHUNK), dtype=bool))[None, None, :, :, None]
    lmat = jnp.exp(jnp.where(tri, seg, -jnp.inf))
    scores = jnp.einsum('bclhn,bcshn->bclsh', cc, bc) * lmat
    y_diag = jnp.einsum('bclsh,bcshp->bclhp', scores, xc)
    decay_states = jnp.exp(acs[:, :, -1:, :] - acs)
    states = jnp.einsum('bcshn,bcsh,bcshp->bchpn', bc, decay_states, xc)
    chunk_decay = jnp.exp(acs[:, :, -1, :])

    def step(carry, inp):
        s_c, d_c = inp
        new = d_c[:, :, None, None] * carry + s_c
        return new, carry

    init = jnp.zeros((b, h, p, n), jnp.float32)
    _, prev = lax.scan(step, init, (states.transpose(1, 0, 2, 3, 4), chunk_decay.transpose(1, 0, 2)))
    prev = prev.transpose(1, 0, 2, 3, 4)
    y_off = jnp.einsum('bclhn,bchpn,bclh->bclhp', cc, prev, jnp.exp(acs))
    return (y_diag + y_off).reshape(b, l, h, p)

def hybrid_mixer(h, cos, sin, w_in, q_a_norm_w, w_q_up, kv_a_norm_w, w_kv_up,
                 q_nope_norm_w, q_pe_norm_w, k_nope_norm_w, k_pe_norm_w,
                 conv_w, conv_b, dt_bias, a_log, d_skip, ssd_norm_w, w_out):
    b, s, _ = h.shape
    proj = h @ w_in
    cuts = np.cumsum([Q_LORA_RANK, KV_LORA_RANK, QK_ROPE_DIM, D_SSD, D_CONV])
    q_a, kv_a, k_pe, z, xbc, dt_raw = jnp.split(proj, [int(i) for i in cuts], axis=-1)

    q = (rmsnorm_2(q_a, q_a_norm_w) @ w_q_up).reshape(b, s, MLA_HEADS, QK_HEAD_DIM)
    q_nope, q_pe = jnp.split(q, [QK_NOPE_DIM], axis=-1)
    kv = (rmsnorm_2(kv_a, kv_a_norm_w) @ w_kv_up).reshape(b, s, MLA_HEADS, QK_NOPE_DIM + V_HEAD_DIM)
    k_nope, v = jnp.split(kv, [QK_NOPE_DIM], axis=-1)
    q_nope = rmsnorm_2(q_nope, q_nope_norm_w)
    q_pe = rope(rmsnorm_2(q_pe, q_pe_norm_w), cos, sin)
    k_nope = rmsnorm_2(k_nope, k_nope_norm_w)
    k_pe = rope(rmsnorm_2(k_pe[:, :, None, :], k_pe_norm_w), cos, sin)
    q_full = jnp.concatenate([q_nope, q_pe], axis=-1)
    k_full = jnp.concatenate([k_nope, jnp.broadcast_to(k_pe, (b, s, MLA_HEADS, QK_ROPE_DIM))], axis=-1)
    attn_out = causal_attention(q_full.transpose(0, 2, 1, 3), k_full.transpose(0, 2, 1, 3),
                                v.transpose(0, 2, 1, 3))

    xbc = lax.conv_general_dilated(xbc, conv_w[:, None, :], window_strides=(1,),
                                   padding=[(CONV_WIDTH_2 - 1, 0)],
                                   dimension_numbers=('NWC', 'WIO', 'NWC'),
                                   feature_group_count=D_CONV)
    xbc = jax.nn.silu(xbc + conv_b)
    xs, bm, cm = jnp.split(xbc, [D_SSD, D_SSD + SSD_GROUPS * SSD_STATE], axis=-1)
    xs = xs.reshape(b, s, SSD_HEADS, SSD_HEAD_DIM)
    bm = bm.reshape(b, s, SSD_GROUPS, SSD_STATE)
    cm = cm.reshape(b, s, SSD_GROUPS, SSD_STATE)
    dt = jax.nn.softplus(dt_raw.astype(jnp.float32) + dt_bias.astype(jnp.float32))
    a = -jnp.exp(a_log.astype(jnp.float32))
    y = ssd_chunked(xs, dt, a, bm, cm) + d_skip.astype(jnp.float32)[:, None] * xs.astype(jnp.float32)
    y = y.astype(h.dtype).reshape(b, s, D_SSD)
    yg = (y * jax.nn.silu(z)).reshape(b, s, SSD_GROUPS, D_SSD // SSD_GROUPS)
    yg = rmsnorm_2(yg, jnp.ones((D_SSD // SSD_GROUPS,), h.dtype)).reshape(b, s, D_SSD) * ssd_norm_w

    return jnp.concatenate([attn_out, yg], axis=-1) @ w_out

def swiglu(h, w_gate_up, w_down):
    g, u = jnp.split(h @ w_gate_up, 2, axis=-1)
    return (jax.nn.silu(g) * u) @ w_down

def second_inputs(seed: int = 0) -> dict:
    key = jax.random.key(seed)
    ks = jax.random.split(key, 32)
    f32 = jnp.float32

    def nrm(k, shape, scale):
        return jax.random.normal(k, shape, f32) * scale

    def gain(k, shape):
        return 1.0 + 0.05 * jax.random.normal(k, shape, f32)

    L = DEPTH_2
    dt0 = jnp.exp(jax.random.uniform(ks[18], (L, SSD_HEADS), f32, np.log(1e-3), np.log(1e-1)))
    dt_bias = dt0 + jnp.log(-jnp.expm1(-dt0))
    pos_off = jax.random.randint(ks[2], (BATCH, 1), 0, 1024, dtype=jnp.int32)
    return {
        "x": nrm(ks[0], (BATCH, SEQ, D_MODEL), 1.0),
        "c": nrm(ks[1], (BATCH, D_MODEL), 1.0),
        "positions": pos_off + jnp.arange(SEQ, dtype=jnp.int32)[None, :],
        "norm1_w": gain(ks[3], (L, D_MODEL)),
        "norm2_w": gain(ks[4], (L, D_MODEL)),
        "w_ada": nrm(ks[5], (L, D_MODEL, N_MOD * D_MODEL), 0.5 * D_MODEL ** -0.5),
        "b_ada": nrm(ks[6], (L, N_MOD * D_MODEL), 0.01),
        "w_in": nrm(ks[7], (L, D_MODEL, D_IN), D_MODEL ** -0.5),
        "q_a_norm_w": gain(ks[8], (L, Q_LORA_RANK)),
        "w_q_up": nrm(ks[9], (L, Q_LORA_RANK, MLA_HEADS * QK_HEAD_DIM), Q_LORA_RANK ** -0.5),
        "kv_a_norm_w": gain(ks[10], (L, KV_LORA_RANK)),
        "w_kv_up": nrm(ks[11], (L, KV_LORA_RANK, MLA_HEADS * (QK_NOPE_DIM + V_HEAD_DIM)), KV_LORA_RANK ** -0.5),
        "q_nope_norm_w": gain(ks[12], (L, QK_NOPE_DIM)),
        "q_pe_norm_w": gain(ks[13], (L, QK_ROPE_DIM)),
        "k_nope_norm_w": gain(ks[14], (L, QK_NOPE_DIM)),
        "k_pe_norm_w": gain(ks[15], (L, QK_ROPE_DIM)),
        "conv_w": nrm(ks[16], (L, CONV_WIDTH_2, D_CONV), CONV_WIDTH_2 ** -0.5),
        "conv_b": nrm(ks[17], (L, D_CONV), 0.01),
        "dt_bias": dt_bias,
        "a_log": jnp.log(jax.random.uniform(ks[19], (L, SSD_HEADS), f32, 1.0, 16.0)),
        "d_skip": 1.0 + 0.1 * jax.random.normal(ks[20], (L, SSD_HEADS), f32),
        "ssd_norm_w": gain(ks[21], (L, D_SSD)),
        "w_out": nrm(ks[22], (L, D_MIX, D_MODEL), D_MIX ** -0.5),
        "w_gate_up": nrm(ks[23], (L, D_MODEL, 2 * D_FF_2), D_MODEL ** -0.5),
        "w_down": nrm(ks[24], (L, D_FF_2, D_MODEL), D_FF_2 ** -0.5),
    }

def second_block(x, c, positions, norm1_w, norm2_w, w_ada, b_ada, w_in, q_a_norm_w, w_q_up,
              kv_a_norm_w, w_kv_up, q_nope_norm_w, q_pe_norm_w, k_nope_norm_w, k_pe_norm_w,
              conv_w, conv_b, dt_bias, a_log, d_skip, ssd_norm_w, w_out, w_gate_up, w_down):
    inv_freq = 1.0 / (ROPE_THETA ** (jnp.arange(0, QK_ROPE_DIM, 2, dtype=jnp.float32) / QK_ROPE_DIM))
    ang = positions.astype(jnp.float32)[..., None] * inv_freq
    cos = jnp.cos(ang)[:, :, None, :].astype(x.dtype)
    sin = jnp.sin(ang)[:, :, None, :].astype(x.dtype)
    c_act = jax.nn.silu(c)
    for l in range(DEPTH_2):
        mod = (c_act @ w_ada[l] + b_ada[l])[:, None, :]
        sh1, sc1, g1, sh2, sc2, g2 = jnp.split(mod, N_MOD, axis=-1)
        h = rmsnorm_2(x, norm1_w[l]) * (1.0 + sc1) + sh1
        x = x + g1 * hybrid_mixer(h, cos, sin, w_in[l], q_a_norm_w[l], w_q_up[l], kv_a_norm_w[l],
                                  w_kv_up[l], q_nope_norm_w[l], q_pe_norm_w[l], k_nope_norm_w[l],
                                  k_pe_norm_w[l], conv_w[l], conv_b[l], dt_bias[l], a_log[l],
                                  d_skip[l], ssd_norm_w[l], w_out[l])
        h = rmsnorm_2(x, norm2_w[l]) * (1.0 + sc2) + sh2
        x = x + g2 * swiglu(h, w_gate_up[l], w_down[l])
    return x


def setup_inputs(seed=0):
    out = dict(first_inputs(seed))
    for name, value in second_inputs(seed + 1).items():
        if name != "x":
            out[name + "_2"] = value
    return out


def reference(
    x, norm1_g, w_in, conv_dw_w, conv_dw_b, conv_ln_g, conv_ln_b, lru_conv_w, lru_conv_b,
    lru_wa, lru_ba, lru_wx, lru_bx, lru_lambda, w_out, norm2_g, w_up, w_down, final_g, c_2,
    positions_2, norm1_w_2, norm2_w_2, w_ada_2, b_ada_2, w_in_2, q_a_norm_w_2, w_q_up_2,
    kv_a_norm_w_2, w_kv_up_2, q_nope_norm_w_2, q_pe_norm_w_2, k_nope_norm_w_2, k_pe_norm_w_2,
    conv_w_2, conv_b_2, dt_bias_2, a_log_2, d_skip_2, ssd_norm_w_2, w_out_2, w_gate_up_2,
    w_down_2,
):
    x = first_block(
        x, norm1_g, w_in, conv_dw_w, conv_dw_b, conv_ln_g, conv_ln_b, lru_conv_w, lru_conv_b,
        lru_wa, lru_ba, lru_wx, lru_bx, lru_lambda, w_out, norm2_g, w_up, w_down, final_g,
    )
    return second_block(
        x, c_2, positions_2, norm1_w_2, norm2_w_2, w_ada_2, b_ada_2, w_in_2, q_a_norm_w_2,
        w_q_up_2, kv_a_norm_w_2, w_kv_up_2, q_nope_norm_w_2, q_pe_norm_w_2, k_nope_norm_w_2,
        k_pe_norm_w_2, conv_w_2, conv_b_2, dt_bias_2, a_log_2, d_skip_2, ssd_norm_w_2, w_out_2,
        w_gate_up_2, w_down_2,
    )


_drawn_inputs = setup_inputs


def setup_inputs(seed=0):
    import zlib

    import numpy as np

    out = dict(_drawn_inputs(seed))
    spreads = {}
    factors = {'norm1_g': 4.825,
     'conv_dw_b': 4.405,
     'conv_ln_g': 6.868,
     'conv_ln_b': 7.98,
     'lru_ba': 8.0,
     'lru_bx': 8.0,
     'norm2_g': 3.091,
     'final_g': 2.699,
     'norm2_w_2': 2.74,
     'b_ada_2': 3.362,
     'q_a_norm_w_2': 8.0,
     'kv_a_norm_w_2': 7.756,
     'q_nope_norm_w_2': 8.0,
     'q_pe_norm_w_2': 8.0,
     'k_nope_norm_w_2': 8.0,
     'k_pe_norm_w_2': 8.0,
     'conv_b_2': 8.0,
     'd_skip_2': 3.23,
     'ssd_norm_w_2': 4.02}
    for name, (base, spread) in spreads.items():
        noise = np.random.default_rng([zlib.crc32(name.encode()), seed]).standard_normal(out[name].shape)
        drawn = base * np.exp(spread * noise) if base else spread * noise
        out[name] = __import__('jax').numpy.asarray(drawn.astype(out[name].dtype))
    for name, factor in factors.items():
        out[name] = (out[name] * factor).astype(out[name].dtype)
    return out
```

```python
import math
from contextlib import ExitStack

import concourse.bass as bass
from concourse import mybir

F32, F32R, I32 = mybir.dt.float32, mybir.dt.float32r, mybir.dt.int32
ALU, ACT, AX = mybir.AluOpType, mybir.ActivationFunctionType, mybir.AxisListType

P, S, KT = 128, 512, 8
NB = S // P
LAYERS = 2
RING = 4
IN1, OUT1, FF1_GROUPS, FF1 = 19, 8, 4, 16
IN2, UP2, OUT2 = 16, 4, 8
FF2_PAIRS = (8, 8, 6)
FF2 = sum(2 * n + KT for n in FF2_PAIRS)
PANELS_1 = IN1 + OUT1 + FF1_GROUPS * FF1
PANELS_L = IN2 + UP2 + OUT2 + FF2
PANELS = PANELS_1 + LAYERS * PANELS_L + RING
V0 = 13
IN1_TILES = IN1 + 1
TILES_1 = IN1_TILES + OUT1 + FF1_GROUPS * FF1
UP2_TILES = 14
TILES_L = IN2 + UP2_TILES + OUT2 + FF2
ADA_PAIRS, ADA_RING = LAYERS * 6, 4
ADA_PER_GROUP = ADA_PAIRS * KT // FF1_GROUPS
CONV_TAPS, LRU_TAPS, CONV2_TAPS = 31, 4, 4
HEADS2, NOPE, ROPE = 8, 64, 32
SSD_BANKS = (0, 3, 1, 2)

C1 = {}
_n = 0
for _name, _w in (("norm1", 8), ("norm2", 8), ("final", 8), ("conv_w", 62), ("conv_b", 2), ("ln_g", 2), ("ln_b", 2),
                  ("lru_w", 12), ("lru_b", 3), ("ba", 3), ("bx", 3), ("lam", 3), ("c", 8), ("b_ada", 96),
                  ("invf", 1), ("eps6", 1), ("eps5", 1)):
    C1[_name] = _n
    _n += _w
NC1 = _n
C2 = {}
_n = 0
for _name, _w in (("norm1", 8), ("norm2", 8), ("qa", 2), ("kva", 1), ("qn", 1), ("qp", 1), ("kn", 1), ("kp", 1),
                  ("conv_w", 32), ("conv_b", 8), ("dt_b", 1), ("a_log", 1), ("dskip", 4), ("ssd", 4)):
    C2[_name] = _n
    _n += _w
NC2 = _n
LN_EXP = "natural_log_exp_and_others"
CONSTS = ("ident", "ones", "e64", "e32", "rot", "negmask", "keep")


def top_bits(x, bits):
    scale = 2.0 ** (bits - 1 - math.floor(math.log2(x)))
    return math.floor(x * scale) / scale


TWO_PI = []
_rest = 2 * math.pi
for _ in range(3):
    TWO_PI.append(top_bits(_rest, 8))
    _rest -= TWO_PI[-1]
TWO_PI.append(_rest)
ROUND = 1.5 * 2.0 ** 23
PI_BELOW = 3.1415925

DVE_FF1, DVE_LAYER, ACT_LAYER = KT + 3, 71, 18


class Steps:

    def __init__(self, eng, sem):
        self.eng, self.sem, self.n, self.base = eng, sem, 0, 0

    def mark(self, ins):
        ins.then_inc(self.sem, 1)
        self.n += 1
        return self.n

    def need(self, k):
        self.eng.wait_ge(self.sem, self.base + k)

    def link(self, ins):
        self.need(self.mark(ins))

    def turn_ends(self, began, per_turn, turns):
        assert self.n - began == per_turn, (self.n - began, per_turn)
        self.n, self.base = began + per_turn * turns, 0


def num(k, terms=(), d=1):
    out = k // d
    for var, count in terms:
        assert count % d == 0
        out = out + var * (count // d)
    return out


def build_program(nc, ap):
    ctx = ExitStack()
    with ctx:
        def sem(name):
            return ctx.enter_context(nc.semaphore(name))

        BASE, END = 16640, 229344
        at = [BASE]

        def place(name, shape, dt=F32, off=None):
            size = 4 * math.prod(shape[1:])
            if off is None:
                off, at[0] = at[0], at[0] + -(-size // 32) * 32
            assert off + size <= END, (name, off + size - END)
            return nc.alloc_sbuf_tensor_at(name, shape, dt, offset=off)

        T = 4 * S
        raw = place("raw", [P, RING, KT * P])
        whi = place("whi", [P, RING, KT * P], F32R)
        wlo = place("wlo", [P, RING, KT * P], F32R)
        X = place("X", [P, KT, S])
        H0 = at[0]
        hhi = place("hhi", [P, KT, S], F32R)
        hlo = place("hlo", [P, KT, S], F32R)
        G0 = at[0]
        ghi = place("ghi", [P, KT, S], F32R)
        glo = place("glo", [P, KT, S], F32R)
        cst = place("cst", [P, len(CONSTS), P])
        cols = place("cols", [P, NC1])
        lcols = place("lcols", [P, LAYERS, NC2])
        lc = place("lc", [P, NC2])
        mods = place("mods", [P, ADA_PAIRS, KT])
        md = place("md", [P, 6, KT])
        small = place("small", [P, 64])
        tok = place("tok", [P, 6, NB * HEADS2])
        wlru = place("wlru", [P, 6, P])
        cos = place("cos", [P, S])
        sin = place("sin", [P, S])
        ident, ones, e64, e32, rot, negmask, keep = (cst[:, i, :] for i in range(len(CONSTS)))
        fast = place("fast", [P, 2, P], F32R)
        A0 = at[0]
        TAIL = (END - 6 * T) // 32 * 32
        ssq = place("ssq", [P, S], off=TAIL)
        sq = place("sq", [P, 2, S], off=TAIL + T)
        hf = place("hf", [P, 2, S], off=TAIL + 3 * T)
        rstd = place("rstd_t", [P, S], off=TAIL + 5 * T)

        at[0] = A0
        ca = place("ca", [P, 2, S])
        sg = place("sg", [P, 2, S])
        upad = place("upad", [P, 2, S + CONV_TAPS - 1])
        ycv = place("ycv", [P, 2, S])
        lxpad = place("lxpad", [P, 3, S + LRU_TAPS - 1])
        lu = place("lu", [P, 3, S])
        lg = place("lg", [P, 3, S])
        rt = [place(f"rt{i}", [P, S], off=at[0] + i * T) for i in range(3)]
        posi = place("posi", [P, S], I32, off=at[0] + 3 * T)
        q1 = place("q1", [P, 3, S])
        k1 = place("k1", [P, 3, S])
        v1 = place("v1", [P, NB, 3 * P])
        lr = place("lr", [P, 3, S])
        li = place("li", [P, 3, S])
        lt = place("lt", [P, 3, S], off=A0 + 4 * T)
        le = place("le", [P, 3, S], off=A0)
        lnsq = sg
        lnrs = place("lnrs", [P, S], off=A0)
        bias1 = place("bias1", [P, 2, 3, S], off=G0 + 5 * T)
        PW = 10 * P
        p1 = place("p1", [P, 3, PW], off=H0)
        pt1 = place("pt1", [P, 2, PW], off=H0 + 12 * PW)
        actb = place("actb", [P, 2, S], off=A0)
        fv = place("fv", [P, 2, S], off=A0 + 2 * T)
        adaw = place("adaw", [P, ADA_RING, KT * P], off=A0 + 4 * T)
        adac = place("adac", [P, 3, KT * P], off=A0 + 12 * T)

        at[0] = A0
        zt = place("zt", [P, 4, S])
        xs = place("xs", [P, 8, S])
        XP = at[0]
        xpad = place("xpad", [P, 8, S + CONV2_TAPS - 1])
        vt = place("vt", [P, NB, S])
        pb = place("pb", [P, 2, S])
        ptb = place("ptb", [P, 2, S])
        acs = place("acs", [P, S])
        rtmp = place("rtmp", [P, 2, S])
        bt = place("bt", [P, 2, NB, P], off=G0 + 4 * T)
        gt = place("gt", [P, 2, NB, P], off=G0 + 6 * T)
        prev = place("prev", [P, 3, S], off=G0 + 12 * T)
        xdt = place("xdt", [P, NB, S], off=XP)
        xdd = place("xdd", [P, NB, S], off=XP + NB * T)
        sqk, rsk = pb, ptb
        qk = [place(f"qk{i}", [P, S], off=G0 + i * T) for i in range(10)]
        qraw, kvraw, misc, kpe = qk[0:2], qk[2], qk[8], qk[9]
        gtmp = qk[3:8]
        qanhi = place("qanhi", [P, 2, S], F32R, off=G0 + 10 * T)
        qanlo = place("qanlo", [P, 2, S], F32R, off=G0 + 12 * T)
        kvnhi = place("kvnhi", [P, S], F32R, off=G0 + 14 * T)
        kvnlo = place("kvnlo", [P, S], F32R, off=G0 + 15 * T)
        rotated = ((rtmp[:, 0, :], rtmp[:, 1, :]), (qk[0][:], qk[1][:]))
        Q = place("Q", [P, HEADS2, S], off=H0)
        K = place("K", [P, HEADS2, S], off=H0 + 8 * T)
        eb = place("eb", [P, 4, S], off=H0)
        db = place("db", [P, 4, S], off=H0 + 4 * T)
        yt = place("yt", [P, 4, S], off=H0 + 8 * T)
        ysq = place("ysq", [P, 4, S], off=H0 + 12 * T)
        yrs = place("yrs", [P, 2, S], off=H0)


        ps = ctx.enter_context(nc.psum_tensor("ps", [P, 8, S], F32))
        NEGM, SUM, RSUM, LAMC, LTMP, CACT, AEXP, ADAS = 0, 4, 8, 12, 21, 36, 44, 48

        raw_in = [sem(f"raw_in{i}") for i in range(RING)]
        hi_ready, lo_ready = sem("hi_ready"), sem("lo_ready")
        gemm_done, evac = sem("gemm_done"), [sem("evac0"), sem("evac1")]
        x_in = [sem(f"x_in{i}") for i in range(KT // 2)]
        fast_ready = sem("fast_ready")
        cols_in, consts_in, lru_w_in, bias_in, pos_in, out_done = (sem(x) for x in ("cols_in", "consts_in", "lru_w_in", "bias_in", "pos_in", "out_done"))
        ada_in = [sem(f"ada_in{i}") for i in range(ADA_RING)]
        ada_free, ada_turned, cact_ready = (sem(x) for x in ("ada_free", "ada_turned", "cact_ready"))
        dve_step, act_step = sem("dve_step"), sem("act_step")
        sq_new, ssq_new, ss_ps, rstd_new, x_new = (sem(x) for x in ("sq_new", "ssq_new", "ss_ps", "rstd_new", "x_new"))
        hf_new, hhi_new, hlo_new = sem("hf_new"), sem("hhi_new"), sem("hlo_new")
        f_new, g_hi, g_lo = sem("f_new"), sem("g_hi"), sem("g_lo")
        mix_f, mix_hi, mix_new = sem("mix_f"), sem("mix_hi"), sem("mix_new")
        rope_arg, rope_done = sem("rope_arg"), sem("rope_done")
        conv_y, ln_sum, ln_d, ln_sq, ln_var, ln_rs, ln_v = (
            sem(x) for x in ("conv_y", "ln_sum", "ln_d", "ln_sq", "ln_var", "ln_rs", "ln_v"))
        lam_abs, lam_exp, lam_w, lam_ln, lam_done = (sem(x) for x in ("lam_abs", "lam_exp", "lam_w", "lam_ln", "lam_done"))
        lru_u, lru_gates, lru_ri, lru_exps, lru_om, lru_b = (
            sem(x) for x in ("lru_u", "lru_gates", "lru_ri", "lru_exps", "lru_om", "lru_b"))
        at_s, at_bias, at_max, at_exp, at_norm, at_tr, at_pt, at_pv = (
            sem(x) for x in ("at_s", "at_bias", "at_max", "at_exp", "at_norm", "at_tr", "at_pt", "at_pv"))
        bs_s, bs_max, bs_exp, bs_norm, bs_tr, bs_pt, bs_pv = (
            sem(x) for x in ("bs_s", "bs_max", "bs_exp", "bs_norm", "bs_tr", "bs_pt", "bs_pv"))
        lc_ready, lo_sq, lo_ss, lo_rs, lo_hf, lo_hi, lo_lo, kp_n, kp_rot = (
            sem(x) for x in ("lc_ready", "lowrank_sq", "lowrank_ss", "lowrank_rs", "lowrank_hf", "lowrank_hi", "lowrank_lo", "kp_n", "kp_rot"))
        dt_abs, dt_exp, dt_w, dt_ln, dt_ready, tok_tr, tok_copied, last_ps, tok_diff, tok_exp, tok_ready = (
            sem(x) for x in ("dt_abs", "dt_exp", "dt_w", "dt_ln", "dt_ready", "tok_tr", "tok_copied", "last_ps", "tok_diff", "tok_exp", "tok_ready"))
        cv_y, cv_act, l2_done = sem("cv_y"), sem("cv_act"), sem("l2_done")
        qk_sq, qk_ss, qk_rs, qk_out, pe_n, pe_rot, q_pe = (
            sem(x) for x in ("qk_sq", "qk_ss", "qk_rs", "qk_out", "pe_n", "pe_rot", "q_pe"))
        sd_load, sd_evac, sd_yt, sd_abc, sd_e, sd_d, sd_l, sd_m, sd_y, sd_yg, sd_sq, sd_ss, sd_rs, sd_hf = (
            sem("ssd_" + x) for x in ("load", "evac", "yt", "abc", "e", "d", "l", "m", "y", "yg", "sq", "ss", "rs", "hf"))

        block = ctx.enter_context(nc.Block())

        def gemm3(eng, out, hi, lo, rhi, rlo, first, last):
            eng.matmul(out, hi, rhi, start=first, stop=False)
            eng.matmul(out, hi, rlo, start=False, stop=False)
            return eng.matmul(out, lo, rhi, start=False, stop=last)

        PL = lambda l: ((l, PANELS_L),)
        TL = lambda l: ((l, TILES_L),)

        @block.sync
        def _(sp):
            sp.dma_start(cols[:], ap["cols"]).then_inc(cols_in, 16)
            for j in range(0, KT, 2):
                sp.dma_start(X[:, j:j + 2, :], ap["x"][:, j:j + 2, :]).then_inc(x_in[j // 2], 16)
            sp.dma_start(cst[:], ap["consts"]).then_inc(consts_in, 16)
            for n in range(RING):
                sp.dma_start(raw[:, n, :], ap["panels"][n]).then_inc(raw_in[n], 16)
            sp.dma_start(wlru[:], ap["w_lru"]).then_inc(lru_w_in, 16)
            sp.dma_start(lcols[:], ap["lcols"]).then_inc(lru_w_in, 16)
            sp.dma_start(bias1[:], ap["bias"]).then_inc(bias_in, 16)

            def load(slot, n):
                sp.wait_ge(lo_ready, n - RING + 1)
                sp.dma_start(raw[:, slot, :], ap["panels"][n]).then_inc(raw_in[slot], 16)

            with sp.Fori(0, (IN1 + OUT1) // RING - 1) as i:
                for s in range(RING):
                    load(s, i * RING + (RING + s))
            for n in range((IN1 + OUT1) // RING * RING, IN1 + OUT1):
                load(n % RING, n)
            FP = IN1 + OUT1
            with sp.Fori(0, (FF1_GROUPS * FF1 + LAYERS * PANELS_L) // RING) as i:
                for s in range(RING):
                    load((FP + s) % RING, i * RING + (FP + s))
            for n in range(PANELS - RING, PANELS):
                load(n % RING, n)
            for b in range(2):
                sp.wait_ge(evac[b], (TILES_1 + LAYERS * TILES_L - b + 1) // 2)
            sp.dma_start(ap["out"], X[:]).then_inc(out_done, 16)
            sp.wait_ge(out_done, 16)

        @block.gpsimd
        def _(pool):
            pool.dma_start(posi[:], ap["positions"].partition_broadcast(P)).then_inc(pos_in, 16)

            def low(slot, n):
                pool.wait_ge(hi_ready, n + 1)
                pool.tensor_tensor(wlo[:, slot, :], raw[:, slot, :], whi[:, slot, :].bitcast(F32),
                                   ALU.subtract).then_inc(lo_ready, 1)

            with pool.Fori(0, PANELS_1 // RING) as i:
                for s in range(RING):
                    low(s, i * RING + s)
            for n in range(PANELS_1 // RING * RING, PANELS_1):
                low(n % RING, n)
            with pool.Fori(0, LAYERS) as l:
                def lows(first, count):
                    with pool.Fori(0, count // RING) as i:
                        for s in range(RING):
                            low((PANELS_1 + first + s) % RING, l * PANELS_L + i * RING + (PANELS_1 + first + s))

                lows(0, IN2 + UP2)
                for m in range(2):
                    for n in ((20, 21), (22,))[m]:
                        low((PANELS_1 + n) % RING, l * PANELS_L + (PANELS_1 + n))
                    pool.wait_ge(lo_ready, l * PANELS_L + (PANELS_1 + (22, 23)[m]))
                    pool.wait_ge(qk_out, l * 10 + (5 + m))
                    for s in range(4):
                        rows = slice(32 * s, 32 * s + 32)
                        pool.tensor_tensor(Q[64:96, 4 * m + s, :], rotated[m][0][rows, :], rotated[m][1][rows, :],
                                           ALU.add).then_inc(q_pe, 1)
                        pool.wait_ge(q_pe, l * 8 + (4 * m + s + 1))
                low((PANELS_1 + 23) % RING, l * PANELS_L + (PANELS_1 + 23))
                lows(24, PANELS_L - 24)
            for n in range(PANELS - RING, PANELS):
                low(n % RING, n)

        @block.tensor
        def _(pe):
            def split_in(n):
                pe.wait_ge(lo_ready, n + 1)

            def bank_empty(tile):
                b, uses = tile
                pe.wait_ge(evac[b], uses)

            def tile_at(base, terms=()):
                return base % 2, num(base, terms, 2)

            def project(pbase, pterms, tbase, tterms, src, ks=KT, also=None, ready=None):
                slot = pbase % RING
                b, uses = tile_at(tbase, tterms)
                split_in(num(pbase, pterms))
                if also is not None:
                    pe.wait_ge(*also)
                if tbase >= 2:
                    bank_empty((b, uses))
                for i in range(ks):
                    k = i if ready is None else ready[0][i]
                    if ready is not None:
                        pe.wait_ge(*ready[1](i))
                    w = slice(k * P, (k + 1) * P)
                    mm = gemm3(pe, ps[:, b, :], whi[:, slot, w], wlo[:, slot, w], src[0][:, k, :], src[1][:, k, :],
                               i == 0, i == ks - 1)
                mm.then_inc(gemm_done, 1)

            def project_pair(pbase, pterms, tbase, tterms, src, by_tile):
                LAG = 1
                for i in range(KT + LAG):
                    for m, k in ((0, i), (1, i - LAG)):
                        if not 0 <= k < KT:
                            continue
                        if k == 0:
                            split_in(num(pbase + m, pterms))
                            if tbase + m >= 2:
                                bank_empty(tile_at(tbase + m, tterms))
                        if m == 0:
                            pe.wait_ge(*by_tile(k))
                        slot, b, w = (pbase + m) % RING, (tbase + m) % 2, slice(k * P, (k + 1) * P)
                        mm = gemm3(pe, ps[:, b, :], whi[:, slot, w], wlo[:, slot, w], src[0][:, k, :], src[1][:, k, :],
                                   k == 0, k == KT - 1)
                        if k == KT - 1:
                            mm.then_inc(gemm_done, 1)

            def ada_sums(g, j):
                if j in (5, 9, 13):
                    q = (j - 5) // 4
                    pe.wait_ge(ada_free, g * ADA_PER_GROUP + (ADA_RING + KT * (q + 1)))
                    for m in range(KT):
                        mm = pe.transpose(ps[:, 3 + m // 4, m % 4 * P:(m % 4 + 1) * P], adac[:, q, m * P:(m + 1) * P], ident)
                    mm.then_inc(ada_turned, 1)

            def head_sums(per, i):
                pe.wait_ge(qk_sq, per(i + 1, 10))
                if i >= 2:
                    pe.wait_ge(qk_rs, per(i - 1, 10))
                pe.matmul(ps[:, 2 + i % 2, :], e32 if i in (4, 5) else e64, sqk[:, i % 2, :],
                          start=True, stop=True).then_inc(qk_ss, 1)
                if i in (5, 6):
                    pe.wait_ge(pe_n, per(i - 4, 2))
                    pe.matmul(ps[:, 4, :], rot, qk[i - 1][:], start=True, stop=True).then_inc(pe_rot, 1)

            def sum_squares(inst, terms=()):
                pe.wait_ge(ssq_new, num(6 * inst + 6, tuple((v, 6 * c) for v, c in terms)))
                pe.matmul(ps[:, 2, :], ones, ssq[:], start=True, stop=False)
                pe.wait_ge(sq_new, num(KT * inst + KT, tuple((v, KT * c) for v, c in terms)))
                pe.matmul(ps[:, 2, :], ones, sq[:, (KT - 2) % 2, :], start=False, stop=True).then_inc(ss_ps, 1)

            h, gx = (hhi, hlo), (ghi, glo)
            pe.wait_ge(consts_in, 16)
            sum_squares(0)

            project_pair(0, (), 0, (), h, lambda k: (hlo_new, k + 1))
            for n in range(2, V0):
                project(n, (), n, (), h)
            split_in(V0 + 2)
            slots = slice(V0 % RING, V0 % RING + 3)
            for b in range(NB):
                t = V0 + b
                bank_empty((t % 2, t // 2))
                for k in range(KT):
                    tokens, w = slice(b * P, (b + 1) * P), slice(k * P, (k + 1) * P)
                    mm = gemm3(pe, ps[:, t % 2, 0:3 * P].rearrange("p (a b) -> p a b", a=3), hhi[:, k, tokens], hlo[:, k, tokens],
                               whi[:, slots, w], wlo[:, slots, w], k == 0, k == KT - 1)
                mm.then_inc(gemm_done, 1)
                if b == 1:
                    pe.wait_ge(conv_y, 2)
                    for i in range(2):
                        mm = pe.matmul(ps[:, 3, :], ones, ycv[:, i, :], start=i == 0, stop=i == 1)
                    mm.then_inc(ln_sum, 1)
            for n in range(V0 + 3, IN1):
                project(n, (), n + 1, (), h)
                if n == 16:
                    for i in range(2):
                        pe.wait_ge(ln_sq, i + 1)
                        mm = pe.matmul(ps[:, 4, :], ones, lnsq[:, i, :], start=i == 0, stop=i == 1)
                    mm.then_inc(ln_var, 1)
                i = n - 16
                if i == 0:
                    pe.wait_ge(lru_w_in, 32)
                pe.wait_ge(lru_u, i + 1)
                if i:
                    pe.wait_ge(lru_ri, 2 * i)
                for m in range(2):
                    mm = pe.matmul(ps[:, 5 + m, :], wlru[:, 3 * m + i, :], lu[:, i, :], start=True, stop=True)
                mm.then_inc(lru_gates, 1)

            O = (7, 0, 1)
            items1 = 2 * NB

            def blocks1(i):
                b = i % NB
                return [(0, kb) for kb in range(max(0, b - 1), b + 1)] + [(g, kb) for g in (1, 2) for kb in range(b + 1)]

            chunks = [sum(-(-len(blocks1(m)) // 4) for m in range(i)) for i in range(items1 + 1)]

            def scores1(i):
                hh, b = divmod(i, NB)
                r = slice(hh * 64, hh * 64 + 64)
                if i:
                    pe.wait_ge(at_bias, i)
                for g in range(3):
                    n = P * (min(2, b + 1) if g == 0 else b + 1)
                    mm = pe.matmul(ps[:, 2 + g, 0:n], q1[r, g, b * P:(b + 1) * P], k1[r, g, P * (b + 1) - n:P * (b + 1)],
                                   start=True, stop=True)
                mm.then_inc(at_s, 1)

            def transposed1(i):
                blocks = blocks1(i)
                pe.wait_ge(at_norm, i + 1)
                for c in range(0, len(blocks), 4):
                    chunk = chunks[i] + c // 4
                    if chunk >= 2:
                        pe.wait_ge(at_pt, chunk - 1)
                    for m in range(c, min(c + 4, len(blocks))):
                        mm = pe.transpose(ps[:, 5 + chunk % 2, (m - c) * P:(m - c + 1) * P],
                                          p1[:, i % 3, m * P:(m + 1) * P], ident)
                    mm.then_inc(at_tr, 1)

            def values1(i):
                hh, b = divmod(i, NB)
                pe.wait_ge(at_pt, chunks[i + 1])
                for m, (g, kb) in enumerate(blocks1(i)):
                    first = kb == (max(0, b - 1) if g == 0 else 0)
                    mm = pe.matmul(ps[hh * 64:hh * 64 + 64, O[g], b * P:(b + 1) * P], v1[:, kb, g * P + hh * 64:g * P + hh * 64 + 64],
                                   pt1[:, i % 2, m * P:(m + 1) * P], start=first, stop=kb == b)
                mm.then_inc(at_pv, 1)

            for b in range(2):
                pe.wait_ge(evac[b], (IN1_TILES + 1 - b) // 2)
            pe.wait_ge(ln_rs, 1)
            scores1(0)
            pe.wait_ge(lru_ri, 6)
            scores1(1)
            for i in range(items1):
                if i + 2 < items1:
                    scores1(i + 2)
                transposed1(i)
                if i:
                    values1(i - 1)
            values1(items1 - 1)

            made = (3, 4, 5, 6, 7, 1, 2, 0)
            pe.wait_ge(mix_new, 6)
            for j in range(OUT1):
                project(IN1 + j, (), IN1_TILES + j, (), gx, ready=(made, lambda i: (mix_new, i + 1)) if j == 0 else None)
            sum_squares(1)
            FP, FT = IN1 + OUT1, IN1_TILES + OUT1
            with pe.Fori(0, FF1_GROUPS) as g:
                it = ((g, FF1),)
                project_pair(FP, it, FT, it, h, lambda k: (hlo_new, KT + k + 1))
                for j in range(2, KT):
                    project(FP + j, it, FT + j, it, h)
                    ada_sums(g, j)
                for j in range(KT):
                    project(FP + KT + j, it, FT + KT + j, it, gx,
                            ready=(range(KT), lambda k: (g_lo, g * KT + (k + 1))) if j == 0 else None)
                    ada_sums(g, KT + j)
            sum_squares(1 + FF1_GROUPS)
            sum_squares(2 + FF1_GROUPS)

            with pe.Fori(0, LAYERS) as l:
                def per(k, count):
                    return num(k, ((l, count),))

                project_pair(PANELS_1, PL(l), TILES_1, TL(l), h, lambda k: (hlo_new, per(2 * KT + k + 1, 2 * KT)))
                for n in range(2, IN2):
                    project(PANELS_1 + n, PL(l), TILES_1 + n, TL(l), h,
                            also={8: (kp_n, per(1, 1)), 10: (dt_ready, per(1, 1))}.get(n))
                    if n == 4:
                        pe.wait_ge(lo_sq, per(3, 3))
                        for m in range(2):
                            pe.matmul(ps[:, 3 + m, :], ones, gtmp[m][:], start=True, stop=True).then_inc(lo_ss, 1)
                        pe.matmul(ps[0:32, 5, :], e32[0:32, 0:32], gtmp[2][0:32, :], start=True, stop=True).then_inc(lo_ss, 1)
                    if n == 8:
                        pe.matmul(ps[0:32, 6, :], rot[0:32, 0:32], kpe[0:32, :], start=True, stop=True).then_inc(kp_rot, 1)
                    if n == 10:
                        for b in range(NB):
                            for m, t in enumerate((misc, acs)):
                                mm = pe.transpose(ps[:, 7, m * 32 + b * 8:m * 32 + b * 8 + 8], t[32:40, b * P:(b + 1) * P],
                                                  ident[32:40, 32:40])
                        mm.then_inc(tok_tr, 1)
                    if n == 12:
                        pe.wait_ge(tok_copied, per(1, 1))
                        pe.matmul(ps[:, 7, 64:96], ident[:, P - 1:P].broadcast_to([P, P]), tok[:, 1, :],
                                  start=True, stop=True).then_inc(last_ps, 1)

                UP = PANELS_1 + IN2
                UT = TILES_1 + IN2
                for i in range(10):
                    pn, slot = UP + i // 2 if i < 6 else UP + 3, 0
                    slot = pn % RING
                    b, uses = tile_at(UT + i, TL(l))
                    split_in(num(pn, PL(l)))
                    bank_empty((b, uses))
                    if i < 6:
                        pe.wait_ge(lo_lo, per(2, 3))
                        for k in range(2):
                            w = slice(((i % 2) * 2 + k) * P, ((i % 2) * 2 + k + 1) * P)
                            mm = gemm3(pe, ps[:, b, :], whi[:, slot, w], wlo[:, slot, w], qanhi[:, k, :], qanlo[:, k, :],
                                       k == 0, k == 1)
                    else:
                        pe.wait_ge(lo_lo, per(3, 3))
                        w = slice((i - 6) * P, (i - 5) * P)
                        mm = gemm3(pe, ps[:, b, :], whi[:, slot, w], wlo[:, slot, w], kvnhi[:], kvnlo[:], True, True)
                    mm.then_inc(gemm_done, 1)
                    if i:
                        head_sums(per, i - 1)
                slot = (UP + 3) % RING
                for t in range(NB):
                    if t == 2:
                        head_sums(per, 9)
                    b, uses = tile_at(UT + 10 + t, TL(l))
                    bank_empty((b, uses))
                    tokens = slice(t * P, (t + 1) * P)
                    gemm3(pe, ps[:, b, :], kvnhi[:, tokens], kvnlo[:, tokens], whi[:, slot, S:2 * S], wlo[:, slot, S:2 * S],
                          True, True).then_inc(gemm_done, 1)

                items = HEADS2 * NB
                for b in range(2):
                    pe.wait_ge(evac[b], num((UT + UP2_TILES + 1 - b) // 2 * 2, TL(l), 2))

                def scores2(i):
                    hd, b = divmod(i, NB)
                    if i == 0:
                        pe.wait_ge(fast_ready, 1)
                    if b == 0 and hd % 4 == 0:
                        pe.wait_ge(q_pe, per(4 + hd, 8))
                    if b == 0 and hd % 2 == 0:
                        pe.wait_ge(qk_out, per(7 + hd // 2, 10))
                    if i >= 3:
                        pe.wait_ge(bs_exp, per(i - 2, items))
                    pe.matmul(ps[:, 1 + i % 3, 0:(b + 1) * P], Q[0:96, hd, b * P:(b + 1) * P], K[0:96, hd, 0:(b + 1) * P],
                              start=True, stop=False)
                    pe.matmul(ps[:, 1 + i % 3, b * P:(b + 1) * P], fast[:, 0, :], fast[:, 1, :],
                              start=False, stop=True).then_inc(bs_s, 1)

                def transposed2(i):
                    pe.wait_ge(bs_norm, per(i + 1, items))
                    if i >= 2:
                        pe.wait_ge(bs_pt, per(i - 1, items))
                    for kb in range(i % NB + 1):
                        mm = pe.transpose(ps[:, 4 + i % 2, kb * P:(kb + 1) * P], pb[:, i % 2, kb * P:(kb + 1) * P], ident)
                    mm.then_inc(bs_tr, 1)

                def values2(i):
                    hd, b = divmod(i, NB)
                    pe.wait_ge(bs_pt, per(i + 1, items))
                    r = slice((hd % 2) * 64, (hd % 2) * 64 + 64)
                    if i % 8 == 0 and hd >= 4:
                        pe.wait_ge(mix_new, per(8 + hd // 2 - 1, 8))
                    for kb in range(b + 1):
                        mm = pe.matmul(ps[r, 6 + (hd // 2) % 2, b * P:(b + 1) * P], vt[:, kb, hd * 64:hd * 64 + 64],
                                       ptb[:, i % 2, kb * P:(kb + 1) * P], start=kb == 0, stop=kb == b)
                    mm.then_inc(bs_pv, 1)

                def x_tokens(c):
                    for t in range(4):
                        mm = pe.transpose(ps[:, 0, t * P:(t + 1) * P], xs[:, t, c * P:(c + 1) * P], ident)
                    return mm

                def b_tokens(gr):
                    for c in range(NB):
                        mm = pe.transpose(ps[:, 0, c * P:(c + 1) * P], xs[:, 4 + gr, c * P:(c + 1) * P], ident)
                    return mm

                def b_times_c(gr):
                    for c in range(NB):
                        w = slice(c * P, (c + 1) * P)
                        mm = pe.matmul(ps[:, 0, w], xs[:, 4 + gr, w], xs[:, 6 + gr, w], start=True, stop=True)
                    return mm

                def states(c):
                    for gr in range(2):
                        w = slice(gr * 256, gr * 256 + 256)
                        mm = pe.matmul(ps[:, 0, w], bt[:, gr, c, :], xdd[:, c, w], start=True, stop=True)
                    return mm

                loads = [(x_tokens, c) for c in range(NB)] + [(b_tokens, g) for g in range(2)] + \
                        [(b_times_c, g) for g in range(2)] + [(states, c) for c in range(NB - 1)]

                def ssd_load(k):
                    if k == 0:
                        pe.wait_ge(tok_ready, per(1, 1))
                        pe.wait_ge(cv_act, per(8, 8))
                    else:
                        pe.wait_ge(sd_evac, per(k, 11))
                    f, which = loads[k]
                    f(which).then_inc(sd_load, 1)

                def sums_of_head(hd):
                    if hd == 0:
                        pe.wait_ge(sd_evac, per(11, 11))
                    elif hd < 4:
                        pe.wait_ge(bs_exp, per((30, 31, 32)[hd - 1], items))
                    if hd >= 4:
                        pe.wait_ge(sd_d, per(hd - 3, HEADS2))
                    pe.matmul(ps[:, SSD_BANKS[hd % 4], :], ident[32:40, 32 + hd:33 + hd].broadcast_to([8, P]), acs[32:40, :],
                              start=True, stop=True).then_inc(sd_abc, 1)

                for i in range(3):
                    scores2(i)
                for i in range(items):
                    if i + 3 < items:
                        scores2(i + 3)
                    if i >= items - 3:
                        sums_of_head(i - (items - 3))
                    transposed2(i)
                    if i % 2 == 0 and 2 <= i < 24:
                        ssd_load(i // 2 - 1)
                    if i:
                        values2(i - 1)
                values2(items - 1)

                for hd in range(HEADS2):
                    if hd + 3 < HEADS2:
                        sums_of_head(hd + 3)
                    pe.wait_ge(sd_m, per(hd + 1, HEADS2))
                    t = hd // 2
                    if hd in (0, 2):
                        pe.wait_ge(mix_new, per(8 + 3 + t, 8))
                    if t >= 2 and hd % 2 == 0:
                        pe.wait_ge(sd_yt, per(t - 1, 4))
                    out = ps[(hd % 2) * 64:(hd % 2) * 64 + 64, 6 + t % 2, :]
                    for c in range(NB):
                        w = slice(c * P, (c + 1) * P)
                        mm = pe.matmul(out[:, w], xdt[:, c, hd * 64:hd * 64 + 64], db[:, hd % 4, w], start=True, stop=c == 0)
                        if c:
                            mm = pe.matmul(out[:, w], prev[:, c - 1, hd * 64:hd * 64 + 64], eb[:, hd % 4, w],
                                           start=False, stop=True)
                    mm.then_inc(sd_y, 1)
                for gr in range(2):
                    pe.wait_ge(sd_sq, per(2 * gr + 2, 4))
                    for i in range(2):
                        mm = pe.matmul(ps[:, 4 + gr, :], ones, ysq[:, 2 * gr + i, :], start=i == 0, stop=i == 1)
                    mm.then_inc(sd_ss, 1)

                OP, OT = UP + UP2, UT + UP2_TILES
                for j in range(OUT2):
                    project(OP + j, PL(l), OT + j, TL(l), gx,
                            ready=(range(KT), lambda k: (mix_new, per(8 + k + 1, 8))) if j == 0 else None)
                sum_squares(7, ((l, 4),))

                def mlp(done, tp, tt, pairs, lo_base):
                    project_pair(OP + OUT2 + done, tp, OT + OUT2 + done, tt, h, lambda k: (hlo_new, per(3 * KT + k + 1, 2 * KT)))
                    for j in range(2, 2 * pairs):
                        project(OP + OUT2 + done + j, tp, OT + OUT2 + done + j, tt, h)
                    for j in range(KT):
                        project(OP + OUT2 + done + 2 * pairs + j, tp, OT + OUT2 + done + 2 * pairs + j, tt, gx, ks=pairs,
                                ready=(range(pairs), lambda k: (g_lo, lo_base + (k + 1))) if j == 0 else None)

                GLO = FF1_GROUPS * KT
                with pe.Fori(0, 2) as g:
                    mlp(0, PL(l) + ((g, 24),), TL(l) + ((g, 24),), 8, num(GLO, ((l, 22), (g, 8))))
                mlp(48, PL(l), TL(l), 6, num(GLO + 16, ((l, 22),)))
                sum_squares(10, ((l, 4),))

        @block.scalar
        def _(act):
            step = Steps(act, act_step)

            def activate(out, in_, f, **kw):
                return act.activation(out, in_, f, **kw)

            def split_hi(pbase, pterms=()):
                slot = pbase % RING
                act.wait_ge(raw_in[slot], num(pbase // RING * RING, pterms, RING) * 16 + 16)
                activate(whi[:, slot, :], raw[:, slot, :], ACT.Copy).then_inc(hi_ready, 1)

            def evacuate(out, tbase, tterms=(), f=ACT.Copy, width=S, **kw):
                act.wait_ge(gemm_done, num(tbase + 1, tterms))
                activate(out, ps[:, tbase % 2, 0:width], f, **kw).then_inc(evac[tbase % 2], 1)

            def residual_tile(tbase, tterms=()):
                act.wait_ge(evac[tbase % 2], num(tbase // 2 * 2 + 2, tterms, 2))

            def square_x(j, inst, terms, sums):
                six = tuple((v, 6 * c) for v, c in terms)
                if j == 0:
                    if inst:
                        act.wait_ge(ssq_new, num(6 * inst, six))
                        act.wait_ge(ss_ps, sums)
                    out = ssq[:]
                else:
                    if j >= 3:
                        act.wait_ge(ssq_new, num(6 * inst + j - 2, six))
                    out = sq[:, (j - 1) % 2, :]
                activate(out, X[:, j, :], ACT.Square).then_inc(sq_new, 1)

            def inverse_root(out, in_, scale, eps, signal):
                r = slice(in_.start_partition(), in_.start_partition() + in_.shape[0])
                step.link(activate(out, in_, ACT.Ln, scale=scale, bias=cols[r, eps:eps + 1]))
                activate(out, out, ACT.Exp, scale=-0.5).then_inc(signal, 1)

            def norm_root(m):
                act.wait_ge(ss_ps, m)
                inverse_root(rstd[:], ps[:, 2, :], 1.0 / (KT * P), C1["eps6"], rstd_new)

            def normed_hi(first, shift=None):
                for j in range(KT):
                    act.wait_ge(hf_new, first + j + 1)
                    if shift is None:
                        activate(hhi[:, j, :], hf[:, j % 2, :], ACT.Copy).then_inc(hhi_new, 1)
                    else:
                        activate(hhi[:, j, :], hf[:, j % 2, :], ACT.Identity, bias=md[:, shift, j:j + 1]).then_inc(hhi_new, 1)

            act.wait_ge(cols_in, 16)
            activate(small[:, CACT:CACT + KT], cols[:, C1["c"]:C1["c"] + KT], ACT.Silu).then_inc(cact_ready, 1)
            for j in range(KT):
                if j % 2 == 0:
                    act.wait_ge(x_in[j // 2], 16)
                square_x(j, 0, (), 0)
            act.wait_ge(consts_in, 16)
            activate(fast[:, 0, :], ident, ACT.Copy)
            activate(fast[:, 1, :], negmask, ACT.Copy).then_inc(fast_ready, 1)
            split_hi(0)
            split_hi(1)
            act.preload_act_table_set(LN_EXP)
            norm_root(1)
            normed_hi(0)
            split_hi(2)
            split_hi(3)
            act.wait_ge(lam_abs, 1)
            lam = small[:, LTMP:LTMP + 3]
            activate(small[:, LTMP + 3:LTMP + 6], lam, ACT.Exp, scale=-1.0).then_inc(lam_exp, 1)
            act.wait_ge(lam_w, 1)
            activate(small[:, LTMP + 9:LTMP + 12], small[:, LTMP + 6:LTMP + 9], ACT.Ln).then_inc(lam_ln, 1)
            into = ([(ca[:, 0, :], ACT.Copy, 1.0), (sg[:, 0, :], ACT.Sigmoid, 1.0), (ca[:, 1, :], ACT.Copy, 1.0),
                     (sg[:, 1, :], ACT.Sigmoid, 1.0)] + [(lxpad[:, i, LRU_TAPS - 1:], ACT.Copy, 1.0) for i in range(3)]
                    + [(q1[:, i, :], ACT.Copy, 0.125) for i in range(3)] + [(lg[:, i, :], ACT.Gelu_apprx_tanh, 1.0) for i in range(3)]
                    + [(v1[:, i, :], ACT.Copy, 1.0) for i in range(NB)] + [(k1[:, i, :], ACT.Copy, 1.0) for i in range(3)])
            for n, (out, f, scale) in enumerate(into):
                values = V0 <= n < V0 + NB
                evacuate(out, n, f=f, scale=scale, width=3 * P if values else S)
                if n < V0:
                    split_hi(n + RING)
                elif n >= V0 + NB:
                    split_hi(n - 1 + RING)
                elif n == V0 + NB - 1:
                    for m in range(3):
                        split_hi(V0 + m + RING)
                if n == 3:
                    for i, t in enumerate((sin, cos)):
                        act.wait_ge(rope_arg, i + 1)
                        activate(t[:], t[:], ACT.Sin).then_inc(rope_done, 1)
                if n == 16:
                    for i in range(2):
                        act.wait_ge(ln_d, i + 1)
                        activate(lnsq[:, i, :], ycv[:, i, :], ACT.Square).then_inc(ln_sq, 1)
                if n == 17:
                    act.preload_act_table_set(LN_EXP)
                    act.wait_ge(ln_var, 1)
                    inverse_root(lnrs[:], ps[:, 4, :], 1.0 / 256, C1["eps5"], ln_rs)
                if n == 18:
                    for i in range(2):
                        act.wait_ge(ln_v, i + 1)
                        step.link(activate(ycv[:, i, :], ycv[:, i, :], ACT.Silu, bias=cols[:, C1["ln_b"] + i:C1["ln_b"] + i + 1]))
                        activate(ghi[:, 3 + i, :], ycv[:, i, :], ACT.Copy).then_inc(mix_hi, 1)
                if n >= 17:
                    i = n - 17
                    act.wait_ge(lru_gates, i + 1)
                    activate(lr[:, i, :], ps[:, 5, :], ACT.Sigmoid, bias=cols[:, C1["ba"] + i:C1["ba"] + i + 1]).then_inc(lru_ri, 1)
                    activate(li[:, i, :], ps[:, 6, :], ACT.Sigmoid, bias=cols[:, C1["bx"] + i:C1["bx"] + i + 1]).then_inc(lru_ri, 1)

            def lru_decays():
                act.wait_ge(mix_new, 2)
                act.wait_ge(lam_done, 1)
                for i in range(3):
                    c = [small[:, LAMC + 3 * m + i:LAMC + 3 * m + i + 1] for m in range(3)]
                    activate(lt[:, i, :], lr[:, i, :], ACT.Tanh, scale=c[0])
                    activate(le[:, i, :], lr[:, i, :], ACT.Exp, scale=c[1])
                    activate(lr[:, i, :], lr[:, i, :], ACT.Exp, scale=c[2]).then_inc(lru_exps, 1)

            def lru_roots():
                for i in range(3):
                    act.wait_ge(lru_om, i + 1)
                    activate(lt[:, i, :], lt[:, i, :], ACT.Sqrt).then_inc(lru_b, 1)

            def lru_his():
                for i in range(3):
                    act.wait_ge(mix_f, i + 1)
                    activate(ghi[:, 5 + i, :], lg[:, i, :], ACT.Copy).then_inc(mix_hi, 1)

            chunk = 0

            def exp1(i):
                n = P * (min(2, i % NB + 1) + 2 * (i % NB + 1))
                c = i % 4
                act.wait_ge(at_max, i + 1)
                activate(p1[:, i % 3, 0:n], p1[:, i % 3, 0:n], ACT.Exp, bias=small[:, NEGM + c:NEGM + c + 1],
                         accum_out=small[:, SUM + c:SUM + c + 1]).then_inc(at_exp, 1)

            act.preload_act_table_set("exp_and_others")
            exp1(0)
            for i in range(2 * NB):
                if i + 1 < 2 * NB:
                    exp1(i + 1)
                n = P * (min(2, i % NB + 1) + 2 * (i % NB + 1))
                if i >= 2:
                    act.wait_ge(at_pv, i - 1)
                for c in range(0, n, S):
                    act.wait_ge(at_tr, chunk + 1)
                    w = min(S, n - c)
                    activate(pt1[:, i % 2, c:c + w], ps[:, 5 + chunk % 2, 0:w], ACT.Copy).then_inc(at_pt, 1)
                    chunk += 1
                if i == 0:
                    lru_decays()
                if i == 2:
                    lru_roots()
                if i == 2 * NB - 1:
                    lru_his()
            act.preload_act_table_set(LN_EXP)
            act.wait_ge(at_pv, 2 * NB)
            for g, b in ((1, 0), (2, 1), (0, 7)):
                activate(ghi[:, g, :], ps[:, b, :], ACT.Copy).then_inc(mix_hi, 1)
            for j in range(OUT1):
                residual_tile(IN1_TILES + j)
                square_x(j, 1, (), 1)
                split_hi(IN1 + j + RING)
                act.wait_ge(hf_new, KT + j + 1)
                activate(hhi[:, j, :], hf[:, j % 2, :], ACT.Copy).then_inc(hhi_new, 1)
            norm_root(2)
            FP, FT = IN1 + OUT1, IN1_TILES + OUT1

            with act.Fori(0, FF1_GROUPS) as g:
                it = ((g, FF1),)

                def ada_chunks(j):
                    for i in range(2 * j, min(2 * j + 2, ADA_PER_GROUP)):
                        c = g * ADA_PER_GROUP + i
                        act.wait_ge(ada_free, c + 1)
                        act.dma_start(adaw[:, i % ADA_RING, :], ap["w_ada"][c]).then_inc(ada_in[i % ADA_RING], 16)

                ada_chunks(0)

                def hidden_hi(j):
                    act.wait_ge(f_new, g * KT + (j + 1))
                    activate(ghi[:, j, :], fv[:, j % 2, :], ACT.Copy).then_inc(g_hi, 1)

                for j in range(KT):
                    if j >= 2:
                        act.wait_ge(f_new, g * KT + (j - 1))
                    evacuate(actb[:, j % 2, :], FT + j, it, f=ACT.Relu)
                    if j:
                        hidden_hi(j - 1)
                    split_hi(FP + j + RING, it)
                    ada_chunks(j + 1)
                hidden_hi(KT - 1)
                for j in range(KT):
                    residual_tile(FT + KT + j, it)
                    square_x(j, 2, ((g, 1),), 2)
                    split_hi(FP + KT + j + RING, it)
                    ada_chunks(KT + j + 1)

            norm_root(3)
            for j in range(KT):
                act.wait_ge(x_new, j + 1)
                square_x(j, 6, (), 3)

            began = step.n
            with act.Fori(0, LAYERS) as l:
                step.base = l * ACT_LAYER

                def per(k, count):
                    return num(k, ((l, count),))

                L0, T0 = PANELS_1, TILES_1
                act.wait_ge(ss_ps, per(4, 2))
                inverse_root(rstd[:], ps[:, 2, :], 1.0 / (KT * P), C1["eps6"], rstd_new)
                act.wait_ge(lc_ready, per(1, 1))
                step.link(activate(small[32:40, AEXP:AEXP + 1], lc[32:40, C2["a_log"]:C2["a_log"] + 1], ACT.Exp))
                normed_hi(per(2 * KT, 2 * KT), shift=0)

                into = ([(qraw[0][:], ACT.Copy), (qraw[1][:], ACT.Copy), (kvraw[:], ACT.Copy), (misc[:], ACT.Copy)]
                        + [(xpad[:, i, CONV2_TAPS - 1:], ACT.Copy) for i in range(8)] + [(zt[:, i, :], ACT.Silu) for i in range(4)])
                for n, (out, f) in enumerate(into):
                    evacuate(out, T0 + n, TL(l), f=f)
                    if n < IN2 - 1:
                        split_hi(L0 + n + RING, PL(l))
                    if n == 5:
                        for m in range(3):
                            act.wait_ge(lo_ss, per(m + 1, 3))
                            r = slice(0, 32) if m == 2 else slice(0, P)
                            inverse_root(gtmp[m][r, :], ps[r, 3 + m, :], (1.0 / 256, 1.0 / 128, 1.0)[m], C1["eps6"], lo_rs)
                        act.wait_ge(dt_abs, per(1, 1))
                        activate(gtmp[4][32:40, :], gtmp[4][32:40, :], ACT.Exp, scale=-1.0).then_inc(dt_exp, 1)
                    if n == 6:
                        for m, (hi, src) in enumerate(((qanhi[:, 0, :], qraw[0]), (qanhi[:, 1, :], qraw[1]), (kvnhi[:], kvraw))):
                            act.wait_ge(lo_hf, per(m + 1, 3))
                            activate(hi, src[:], ACT.Copy).then_inc(lo_hi, 1)
                        act.wait_ge(dt_w, per(1, 1))
                        activate(acs[32:40, :], gtmp[2][32:40, :], ACT.Ln).then_inc(dt_ln, 1)
                    if 12 <= n < 15:
                        for i in {12: (0, 1, 2, 3), 13: (4, 5), 14: (6, 7)}[n]:
                            act.wait_ge(cv_y, per(i + 1, 8))
                            activate(xs[:, i, :], xs[:, i, :], ACT.Silu,
                                     bias=lc[:, C2["conv_b"] + i:C2["conv_b"] + i + 1]).then_inc(cv_act, 1)
                    if n == 13:
                        act.wait_ge(tok_diff, per(1, 1))
                        activate(tok[:, 2, :], tok[:, 2, :], ACT.Exp)
                        activate(tok[:, 3, :], ps[:, 7, 64:96], ACT.Exp).then_inc(tok_exp, 1)

                act.preload_act_table_set(LN_EXP)
                U0, UT = L0 + IN2, T0 + IN2
                act.wait_ge(tok_ready, per(1, 1))

                def head_root(i):
                    act.wait_ge(qk_ss, per(i + 1, 10))
                    if i >= 2:
                        act.wait_ge(qk_out, per(i - 1, 10))
                    inverse_root(rsk[:, i % 2, :], ps[:, 2 + i % 2, :], 1.0, C1["eps6"], qk_rs)

                for i in range(10):
                    if i == 9:
                        act.wait_ge(l2_done, per(1, 1))
                    evacuate(qk[i][:], UT + i, TL(l))
                    if i == 0:
                        split_hi(L0 + IN2 - 1 + RING, PL(l))
                    if i in (1, 3, 5):
                        split_hi(U0 + i // 2 + RING, PL(l))
                    if i:
                        head_root(i - 1)
                for t in range(NB):
                    if t == 2:
                        head_root(9)
                    evacuate(vt[:, t, :], UT + 10 + t, TL(l))
                split_hi(U0 + 3 + RING, PL(l))

                items = HEADS2 * NB

                def exp2(i):
                    n, c = P * (i % NB + 1), i % 4
                    act.wait_ge(bs_max, per(i + 1, items))
                    if i >= 2:
                        act.wait_ge(bs_tr, per(i - 1, items))
                    activate(pb[:, i % 2, 0:n], ps[:, 1 + i % 3, 0:n], ACT.Exp, bias=small[:, NEGM + c:NEGM + c + 1],
                             accum_out=small[:, SUM + c:SUM + c + 1]).then_inc(bs_exp, 1)

                def heads_out(t):
                    if t == 0:
                        act.wait_ge(q_pe, per(8, 8))
                    act.wait_ge(bs_pv, per(8 * t + 8, items))
                    activate(ghi[:, t, :], ps[:, 6 + t % 2, :], ACT.Copy).then_inc(mix_hi, 1)

                def gate_square(t):
                    act.wait_ge(sd_yg, per(t + 1, 4))
                    activate(ysq[:, t, :], yt[:, t, :], ACT.Square).then_inc(sd_sq, 1)

                def decay_in(hd):
                    act.wait_ge(sd_abc, per(hd + 1, HEADS2))
                    if hd >= 4:
                        act.wait_ge(sd_y, per(hd - 3, HEADS2))
                    activate(eb[:, hd % 4, :], ps[:, SSD_BANKS[hd % 4], :], ACT.Exp).then_inc(sd_e, 1)

                def decay_between(hd):
                    act.wait_ge(sd_d, per(hd + 1, HEADS2))
                    activate(db[:, hd % 4, :], db[:, hd % 4, :], ACT.Exp).then_inc(sd_l, 1)

                exp2(0)
                for i in range(items):
                    if i + 1 < items:
                        exp2(i + 1)
                    n = P * (i % NB + 1)
                    act.wait_ge(bs_tr, per(i + 1, items))
                    if i >= 2:
                        act.wait_ge(bs_pv, per(i - 1, items))
                    activate(ptb[:, i % 2, 0:n], ps[:, 4 + i % 2, 0:n], ACT.Copy).then_inc(bs_pt, 1)
                    if i % 8 == 1 and i > 8:
                        heads_out(i // 8 - 1)
                    if i == items - 2:
                        decay_in(0)
                heads_out(3)

                decay_in(1)
                decay_between(0)
                for hd in range(HEADS2):
                    if hd + 2 < HEADS2:
                        decay_in(hd + 2)
                    if hd + 1 < HEADS2:
                        decay_between(hd + 1)
                    if hd % 2 and hd >= 3:
                        gate_square(hd // 2 - 1)
                gate_square(3)
                for gr in range(2):
                    act.wait_ge(sd_ss, per(gr + 1, 2))
                    inverse_root(yrs[:, gr, :], ps[:, 4 + gr, :], 1.0 / 256, C1["eps6"], sd_rs)
                for t in range(4):
                    act.wait_ge(sd_hf, per(t + 1, 4))
                    activate(ghi[:, 4 + t, :], yt[:, t, :], ACT.Copy).then_inc(mix_hi, 1)

                O0, OT = U0 + UP2, UT + UP2_TILES
                act.preload_act_table_set(LN_EXP)
                for j in range(OUT2):
                    residual_tile(OT + j, TL(l))
                    square_x(j, 7, ((l, 4),), per(4, 2))
                    split_hi(O0 + j + RING, PL(l))
                act.wait_ge(ss_ps, per(5, 2))
                inverse_root(rstd[:], ps[:, 2, :], 1.0 / (KT * P), C1["eps6"], rstd_new)
                normed_hi(per(3 * KT, 2 * KT), shift=3)

                F0, FT = O0 + OUT2, OT + OUT2

                def mlp(done, more, pairs, inst, iterms):
                    pt, tt = PL(l) + more, TL(l) + more

                    def product_ready(j):
                        residual_tile(FT + done + 2 * j + 1, tt)

                    def hidden_hi(j):
                        product_ready(j)
                        activate(ghi[:, j, :], fv[:, j % 2, :], ACT.Copy).then_inc(g_hi, 1)

                    for j in range(pairs):
                        if j >= 2:
                            product_ready(j - 2)
                        evacuate(actb[:, j % 2, :], FT + done + 2 * j, tt, f=ACT.Silu)
                        split_hi(F0 + done + 2 * j + RING, pt)
                        if j:
                            hidden_hi(j - 1)
                        act.wait_ge(gemm_done, num(FT + done + 2 * j + 2, tt))
                        split_hi(F0 + done + 2 * j + 1 + RING, pt)
                    hidden_hi(pairs - 1)
                    if not more:
                        act.preload_act_table_set(LN_EXP)
                    for j in range(KT):
                        residual_tile(FT + done + 2 * pairs + j, tt)
                        square_x(j, inst, iterms, per(5, 2))
                        split_hi(F0 + done + 2 * pairs + j + RING, pt)

                with act.Fori(0, 2) as g:
                    mlp(0, ((g, 24),), 8, 8, ((l, 4), (g, 1)))
                mlp(48, (), 6, 10, ((l, 4),))
            step.turn_ends(began, ACT_LAYER, LAYERS)

        @block.vector
        def _(dve):
            step = Steps(dve, dve_step)
            tt, ts, stt = dve.tensor_tensor, dve.tensor_scalar, dve.scalar_tensor_tensor

            def col(name, i=0):
                return cols[:, C1[name] + i:C1[name] + i + 1]

            def wait_evac(t, terms=()):
                dve.wait_ge(evac[t % 2], num(t // 2 * 2 + 2, terms, 2))

            def add_squares(j, inst, terms=()):
                dve.wait_ge(sq_new, num(KT * inst + j + 1, tuple((v, KT * c) for v, c in terms)))
                if j >= 2:
                    dve.wait_ge(ssq_new, num(6 * inst + j - 1, tuple((v, 6 * c) for v, c in terms)))
                tt(ssq[:], ssq[:], sq[:, (j - 1) % 2, :], ALU.add).then_inc(ssq_new, 1)

            def normalize(a, m, gain, shift=None):
                def value(j):
                    if j >= 2:
                        dve.wait_ge(hlo_new, a + j - 1)
                    stt(hf[:, j % 2, :], X[:, j, :], gain(j), rstd[:], ALU.mult, ALU.mult).then_inc(hf_new, 1)

                dve.wait_ge(rstd_new, m)
                value(0)
                for j in range(KT):
                    if j + 1 < KT:
                        value(j + 1)
                    dve.wait_ge(hhi_new, a + j + 1)
                    hi = hhi[:, j, :].bitcast(F32)
                    if shift is None:
                        tt(hlo[:, j, :], hf[:, j % 2, :], hi, ALU.subtract).then_inc(hlo_new, 1)
                    else:
                        stt(hlo[:, j, :], hf[:, j % 2, :], md[:, shift, j:j + 1], hi, ALU.add, ALU.subtract).then_inc(hlo_new, 1)

            def residual(j, t, terms, inst, iterms=(), gate=None):
                if j >= 2:
                    add_squares(j - 1, inst, iterms)
                dve.wait_ge(gemm_done, num(t + 1, terms))
                if gate is None:
                    ins = tt(X[:, j, :], X[:, j, :], ps[:, t % 2, :], ALU.add)
                else:
                    ins = stt(X[:, j, :], ps[:, t % 2, :], md[:, gate, j:j + 1], X[:, j, :], ALU.mult, ALU.add)
                ins.then_inc(evac[t % 2], 1)

            def mix_low(t, value, count):
                dve.wait_ge(mix_hi, count)
                tt(glo[:, t, :], value, ghi[:, t, :].bitcast(F32), ALU.subtract).then_inc(mix_new, 1)

            dve.wait_ge(cols_in, 16)
            dve.memset(upad[:, :, 0:CONV_TAPS - 1], 0.0)
            dve.memset(lxpad[:, :, 0:LRU_TAPS - 1], 0.0).then_inc(ada_free, ADA_RING)
            for j in range(1, KT - 1):
                add_squares(j, 0)

            def sm(i, n=3):
                return small[:, i:i + n]

            lam_a, y, w, ln_w = (sm(LTMP + 3 * i) for i in range(4))
            lam = cols[:, C1["lam"]:C1["lam"] + 3]
            stt(lam_a, lam, -1.0, lam, ALU.mult, ALU.max).then_inc(lam_abs, 1)
            normalize(0, 1, lambda j: col("norm1", j))
            dve.wait_ge(lam_exp, 1)
            ts(w, y, 1.0, None, ALU.add).then_inc(lam_w, 1)
            dve.wait_ge(lam_w, 1)
            step.link(ts(lam_a, w, -1.0, 1e-30, ALU.add, ALU.max))
            step.link(dve.reciprocal(lam_a, lam_a))
            step.link(tt(lam_a, lam_a, y, ALU.mult))
            dve.wait_ge(lam_ln, 1)
            step.link(tt(lam_a, lam_a, ln_w, ALU.mult))
            step.link(stt(w, w, 1.0, y, ALU.is_equal, ALU.mult))
            step.link(tt(lam_a, lam_a, w, ALU.add))
            step.link(ts(y, lam, -1.0, 0.0, ALU.mult, ALU.max))
            step.link(tt(lam_a, lam_a, y, ALU.add))
            for i, f in enumerate((8.0, -16.0, -8.0)):
                ins = ts(sm(LAMC + 3 * i), lam_a, f, None, ALU.mult)
            ins.then_inc(lam_done, 1)

            dve.wait_ge(pos_in, 16)
            ang, k, r = rt[0][:], rt[1][:], rt[2][:]
            step.link(dve.tensor_copy(ang, posi[:]))
            step.link(ts(ang, ang, col("invf"), None, ALU.mult))
            for t, quarter in ((sin, 0.0), (cos, 0.25)):
                step.link(ts(k, ang, 1.0 / (2 * math.pi), quarter, ALU.mult, ALU.add))
                step.link(ts(k, k, ROUND, None, ALU.add))
                step.link(ts(k, k, -ROUND, None, ALU.add))
                for i, part in enumerate(TWO_PI):
                    if i == 0 and quarter:
                        dve.wait_ge(rope_arg, 1)
                    step.link(stt(r, k, -part, r if i else ang, ALU.mult, ALU.add))
                if quarter:
                    step.link(ts(r, r, 2 * math.pi * quarter, None, ALU.add))
                ts(t[:], r, PI_BELOW, -PI_BELOW, ALU.min, ALU.max).then_inc(rope_arg, 1)
            last = [0, 0]

            def tap(i, t):
                if t == 0:
                    wait_evac(2 * i)
                    wait_evac(2 * i + 1)
                    step.link(tt(upad[:, i, CONV_TAPS - 1:], ca[:, i, :], sg[:, i, :], ALU.mult))
                else:
                    step.need(last[i])
                wt = col("conv_w", i * CONV_TAPS + t)
                if t == 0:
                    ins = ts(ycv[:, i, :], upad[:, i, 0:S], wt, col("conv_b", i), ALU.mult, ALU.add)
                else:
                    ins = stt(ycv[:, i, :], upad[:, i, t:t + S], wt, ycv[:, i, :], ALU.mult, ALU.add)
                if t == CONV_TAPS - 1:
                    ins.then_inc(conv_y, 1)
                else:
                    last[i] = step.mark(ins)

            AHEAD = 14
            for t in range(CONV_TAPS + AHEAD):
                if t < CONV_TAPS:
                    tap(0, t)
                if t >= AHEAD:
                    tap(1, t - AHEAD)
            for t in (4, 5, 6):
                wait_evac(t)
            lru_last = [0, 0, 0]
            for t in range(LRU_TAPS):
                for i in range(3):
                    wt = col("lru_w", i * LRU_TAPS + t)
                    if t == 0:
                        ins = ts(lu[:, i, :], lxpad[:, i, 0:S], wt, col("lru_b", i), ALU.mult, ALU.add)
                    else:
                        step.need(lru_last[i])
                        ins = stt(lu[:, i, :], lxpad[:, i, t:t + S], wt, lu[:, i, :], ALU.mult, ALU.add)
                    if t == LRU_TAPS - 1:
                        ins.then_inc(lru_u, 1)
                    else:
                        lru_last[i] = step.mark(ins)
            dve.wait_ge(ln_sum, 1)
            for i in range(2):
                stt(ycv[:, i, :], ps[:, 3, :], -1.0 / 256, ycv[:, i, :], ALU.mult, ALU.add).then_inc(ln_d, 1)
            dve.wait_ge(ln_rs, 1)
            for i in range(2):
                stt(ycv[:, i, :], ycv[:, i, :], col("ln_g", i), lnrs[:], ALU.mult, ALU.mult).then_inc(ln_v, 1)
            for i in range(2):
                mix_low(3 + i, ycv[:, i, :], i + 1)

            def lru_complements():
                for i in range(3):
                    dve.wait_ge(lru_exps, i + 1)
                    stt(lt[:, i, :], le[:, i, :], 1.0, lt[:, i, :], ALU.add, ALU.mult).then_inc(lru_om, 1)

            def lru_inputs():
                for i in range(3):
                    step.link(tt(li[:, i, :], li[:, i, :], lu[:, i, :], ALU.mult))

            def lru_scan(i):
                dve.wait_ge(lru_b, i + 1)
                step.link(tt(lt[:, i, :], lt[:, i, :], li[:, i, :], ALU.mult))
                step.link(dve.tensor_tensor_scan(lu[:, i, :], lr[:, i, :], lt[:, i, :], 0.0, ALU.mult, ALU.add))
                wait_evac(10 + i)
                tt(lg[:, i, :], lg[:, i, :], lu[:, i, :], ALU.mult).then_inc(mix_f, 1)

            def lru_lows():
                for i in range(3):
                    mix_low(5 + i, lg[:, i, :], 3 + i)

            def widths(b):
                return [P * min(2, b + 1), P * (b + 1), P * (b + 1)]

            chunks = [sum(-(-sum(widths(m % NB)) // S) for m in range(i + 1)) for i in range(2 * NB)]

            def biased1(i):
                hh, b = divmod(i, NB)
                dve.wait_ge(at_s, i + 1)
                if i >= 3:
                    dve.wait_ge(at_tr, chunks[i - 3])
                o = 0
                for g, n in enumerate(widths(b)):
                    ins = tt(p1[:, i % 3, o:o + n], ps[:, 2 + g, 0:n], bias1[:, hh, g, S - n:S], ALU.add)
                    o += n
                ins.then_inc(at_bias, 1)
                dve.wait_ge(at_bias, i + 1)
                dve.reduce_max(small[:, NEGM + i % 4:NEGM + i % 4 + 1], p1[:, i % 3, 0:o], AX.X, negate=True).then_inc(at_max, 1)

            dve.wait_ge(bias_in, 16)

            def normed1(i):
                c, n = i % 4, sum(widths(i % NB))
                dve.wait_ge(at_exp, i + 1)
                step.link(dve.reciprocal(sm(RSUM + c, 1), sm(SUM + c, 1)))
                ts(p1[:, i % 3, 0:n], p1[:, i % 3, 0:n], sm(RSUM + c, 1), None, ALU.mult).then_inc(at_norm, 1)

            biased1(0)
            biased1(1)
            normed1(0)
            for i in range(2 * NB):
                if i + 2 < 2 * NB:
                    biased1(i + 2)
                if i + 1 < 2 * NB:
                    normed1(i + 1)
                if i == 0:
                    lru_inputs()
                if i == 1:
                    lru_complements()
                if 3 <= i < 6:
                    lru_scan(i - 3)
                if i == 2 * NB - 1:
                    lru_lows()
            for n, (g, b) in enumerate(((1, 0), (2, 1), (0, 7))):
                mix_low(g, ps[:, b, :], 6 + n)

            def gained_low(j):
                dve.wait_ge(hhi_new, KT + j + 1)
                tt(hlo[:, j, :], hf[:, j % 2, :], hhi[:, j, :].bitcast(F32), ALU.subtract).then_inc(hlo_new, 1)

            for j in range(OUT1):
                residual(j, IN1_TILES + j, (), 1)
                wait_evac(IN1_TILES + j)
                if j >= 2:
                    dve.wait_ge(hlo_new, KT + j - 1)
                ts(hf[:, j % 2, :], X[:, j, :], col("norm2", j), None, ALU.mult).then_inc(hf_new, 1)
                if j:
                    gained_low(j - 1)
            gained_low(OUT1 - 1)
            dve.wait_ge(rstd_new, 2)

            FT = IN1_TILES + OUT1
            dve.wait_ge(cact_ready, 1)
            began = step.n
            with dve.Fori(0, FF1_GROUPS) as g:
                it = ((g, FF1),)
                step.base = g * DVE_FF1

                def ada_step(j):
                    for i in range(2 * j, min(2 * j + 2, ADA_PER_GROUP)):
                        q, ko = divmod(i, KT)
                        dve.wait_ge(ada_in[i % ADA_RING], g * (16 * ADA_PER_GROUP // ADA_RING) + 16 * (i // ADA_RING + 1))
                        ca_ko = small[:, CACT + ko:CACT + ko + 1]
                        if ko == 0:
                            ins = ts(adac[:, q, :], adaw[:, i % ADA_RING, :], ca_ko, None, ALU.mult)
                        else:
                            dve.wait_ge(ada_free, g * ADA_PER_GROUP + (ADA_RING + i))
                            ins = stt(adac[:, q, :], adaw[:, i % ADA_RING, :], ca_ko, adac[:, q, :], ALU.mult, ALU.add)
                        ins.then_inc(ada_free, 1)
                    if j in (6, 10, 14):
                        q = (j - 6) // 4
                        dve.wait_ge(ada_turned, g * 3 + (q + 1))
                        sums = sm(ADAS, KT)
                        step.link(dve.tensor_reduce(sums, ps[:, 3:5, :].rearrange("p a (b n) -> p (a b) n", n=P), AX.X, ALU.add))
                        tt(mods[:, bass.ds(g * 3 + q, 1), :], sums.unsqueeze(1),
                           cols[:, bass.ds(g * (3 * KT) + (C1["b_ada"] + q * KT), KT)].unsqueeze(1), ALU.add)

                def hidden_low(j):
                    dve.wait_ge(g_hi, g * KT + (j + 1))
                    tt(glo[:, j, :], fv[:, j % 2, :], ghi[:, j, :].bitcast(F32), ALU.subtract).then_inc(g_lo, 1)

                for j in range(KT):
                    wait_evac(FT + j, it)
                    if j >= 2:
                        dve.wait_ge(g_lo, g * KT + (j - 1))
                    scaled = actb[:, j % 2, :]
                    step.link(tt(scaled, scaled, rstd[:], ALU.mult))
                    tt(fv[:, j % 2, :], scaled, scaled, ALU.mult).then_inc(f_new, 1)
                    if j:
                        hidden_low(j - 1)
                    if j == KT - 1:
                        hidden_low(j)
                    ada_step(j)
                for j in range(KT):
                    residual(j, FT + KT + j, it, 2, ((g, 1),))
                    ada_step(KT + j)

            step.turn_ends(began, DVE_FF1, FF1_GROUPS)

            dve.wait_ge(rstd_new, 3)
            for j in range(KT):
                stt(X[:, j, :], X[:, j, :], col("final", j), rstd[:], ALU.mult, ALU.mult).then_inc(x_new, 1)
                if j >= 2:
                    add_squares(j - 1, 6)

            dve.wait_ge(rope_done, 2)
            began = step.n
            with dve.Fori(0, LAYERS) as l:
                step.base = l * DVE_LAYER

                def per(k, count):
                    return num(k, ((l, count),))

                def c2(name, i=0, rows=slice(0, P)):
                    return lc[rows, C2[name] + i:C2[name] + i + 1]

                dve.wait_ge(sq_new, per(7 * KT, 4 * KT))
                dve.memset(xpad[:, :, 0:CONV2_TAPS - 1], 0.0)
                dve.tensor_copy(lc[:].unsqueeze(1), lcols[:, bass.ds(l, 1), :])
                step.link(dve.tensor_copy(md[:], mods[:, bass.ds(l * 6, 6), :]))
                for scale, norm in ((1, "norm1"), (4, "norm2")):
                    stt(md[:, scale, :], md[:, scale, :], 1.0, lc[:, C2[norm]:C2[norm] + KT], ALU.add, ALU.mult)
                ts(lc[:, C2["qn"]:C2["qp"] + 1], lc[:, C2["qn"]:C2["qp"] + 1], float(NOPE + ROPE) ** -0.5, None,
                   ALU.mult).then_inc(lc_ready, 1)
                dve.wait_ge(lc_ready, per(1, 1))
                normalize(per(2 * KT, 2 * KT), per(4, 2), lambda j: md[:, 1, j:j + 1], shift=0)

                T0 = TILES_1
                R, KP = slice(32, 40), slice(0, 32)
                wait_evac(T0, TL(l))
                wait_evac(T0 + 1, TL(l))
                for i in range(2):
                    ins = tt(gtmp[3 * i][:], qraw[i][:], qraw[i][:], ALU.mult)
                step.link(ins)
                tt(gtmp[0][:], gtmp[0][:], gtmp[3][:], ALU.add).then_inc(lo_sq, 1)
                wait_evac(T0 + 2, TL(l))
                tt(gtmp[1][:], kvraw[:], kvraw[:], ALU.mult).then_inc(lo_sq, 1)
                wait_evac(T0 + 3, TL(l))
                tt(gtmp[2][KP, :], misc[KP, :], misc[KP, :], ALU.mult).then_inc(lo_sq, 1)
                v, y, w, q = gtmp[3][R, :], gtmp[4][R, :], gtmp[2][R, :], kpe[R, :]
                dve.wait_ge(lo_sq, per(3, 3))
                step.link(ts(v, misc[R, :], c2("dt_b", rows=R), None, ALU.add))
                stt(y, v, -1.0, v, ALU.mult, ALU.max).then_inc(dt_abs, 1)
                low = ((qraw[0], "qa", 0, gtmp[0], qanhi[:, 0, :], qanlo[:, 0, :]),
                       (qraw[1], "qa", 1, gtmp[0], qanhi[:, 1, :], qanlo[:, 1, :]),
                       (kvraw, "kva", 0, gtmp[1], kvnhi[:], kvnlo[:]))
                dve.wait_ge(lo_rs, per(2, 3))
                for t, name, i, rs, hi, lo in low:
                    stt(t[:], t[:], c2(name, i), rs[:], ALU.mult, ALU.mult).then_inc(lo_hf, 1)
                dve.wait_ge(lo_rs, per(3, 3))
                stt(kpe[KP, :], misc[KP, :], c2("kp", rows=KP), gtmp[2][KP, :], ALU.mult, ALU.mult).then_inc(kp_n, 1)
                dve.wait_ge(dt_exp, per(1, 1))
                ts(w, y, 1.0, None, ALU.add).then_inc(dt_w, 1)
                dve.wait_ge(dt_w, per(1, 1))
                step.link(ts(q, w, -1.0, 1e-30, ALU.add, ALU.max))
                step.link(dve.reciprocal(q, q))
                step.link(tt(q, q, y, ALU.mult))
                dve.wait_ge(dt_ln, per(1, 1))
                step.link(tt(q, q, acs[R, :], ALU.mult))
                step.link(stt(w, w, 1.0, y, ALU.is_equal, ALU.mult))
                step.link(tt(q, q, w, ALU.add))
                step.link(stt(misc[R, :], v, 0.0, q, ALU.max, ALU.add))
                step.link(ts(w, misc[R, :], small[R, AEXP:AEXP + 1], -1.0, ALU.mult, ALU.mult))
                for c in range(NB):
                    ins = dve.tensor_tensor_scan(acs[R, c * P:(c + 1) * P], ones[R, :], gtmp[2][R, c * P:(c + 1) * P],
                                                 0.0, ALU.mult, ALU.add)
                ins.then_inc(dt_ready, 1)
                for m, (t, name, i, rs, hi, lo) in enumerate(low):
                    dve.wait_ge(lo_hi, per(m + 1, 3))
                    tt(lo, t[:], hi.bitcast(F32), ALU.subtract).then_inc(lo_lo, 1)

                for i in range(0, 8, 2):
                    last = [0, 0]
                    for t in range(CONV2_TAPS):
                        for m in range(2):
                            if t == 0:
                                wait_evac(T0 + 4 + i + m, TL(l))
                                ins = ts(xs[:, i + m, :], xpad[:, i + m, 0:S], c2("conv_w", (i + m) * CONV2_TAPS), None, ALU.mult)
                            else:
                                step.need(last[m])
                                ins = stt(xs[:, i + m, :], xpad[:, i + m, t:t + S], c2("conv_w", (i + m) * CONV2_TAPS + t),
                                          xs[:, i + m, :], ALU.mult, ALU.add)
                            if t == CONV2_TAPS - 1:
                                ins.then_inc(cv_y, 1)
                            else:
                                last[m] = step.mark(ins)
                    if i == 2:
                        dve.wait_ge(kp_rot, per(1, 1))
                        tt(gtmp[0][KP, :], kpe[KP, :], cos[KP, :], ALU.mult)
                        step.link(tt(gtmp[1][KP, :], ps[KP, 6, :], sin[KP, :], ALU.mult))
                        step.link(tt(kpe[KP, :], gtmp[0][KP, :], gtmp[1][KP, :], ALU.add))
                    if i == 4:
                        dve.wait_ge(tok_tr, per(1, 1))
                        dve.tensor_copy(tok[:, 0:2, :], ps[:, 7, 0:64].rearrange("p (a b) -> p a b", a=2)).then_inc(tok_copied, 1)
                    if i == 6:
                        dve.wait_ge(last_ps, per(1, 1))
                        tt(tok[:, 2, :], ps[:, 7, 64:96], tok[:, 1, :], ALU.subtract).then_inc(tok_diff, 1)
                dve.wait_ge(tok_exp, per(1, 1))
                tt(tok[:, 4, :], tok[:, 2, :], tok[:, 0, :], ALU.mult).then_inc(tok_ready, 1)

                wait_evac(T0 + IN2 - 1, TL(l))
                wait_evac(T0 + IN2 - 2, TL(l))
                dve.tensor_copy(K[64:96, :, :], kpe[KP, :].unsqueeze(1).broadcast_to([32, HEADS2, S])).then_inc(l2_done, 1)
                UT = T0 + IN2

                def head_out(i):
                    dve.wait_ge(qk_rs, per(i + 1, 10))
                    rs = rsk[:, i % 2, :]
                    if i in (4, 5):
                        stt(qk[i][:], qk[i][:], c2("qp"), rs, ALU.mult, ALU.mult).then_inc(pe_n, 1)
                        dve.wait_ge(pe_rot, per(i - 3, 2))
                        parts = rotated[i - 4]
                        tt(parts[0], qk[i][:], cos[:], ALU.mult)
                        ins = tt(parts[1], ps[:, 4, :], sin[:], ALU.mult)
                    else:
                        dest, name, first = (Q, "qn", 2 * i) if i < 4 else (K, "kn", 2 * (i - 6))
                        for s in range(2):
                            rows = slice(64 * s, 64 * s + 64)
                            ins = stt(dest[0:64, first + s, :], qk[i][rows, :], c2(name, rows=rows), rsk[rows, i % 2, :],
                                      ALU.mult, ALU.mult)
                    ins.then_inc(qk_out, 1)

                for i in range(10):
                    wait_evac(UT + i, TL(l))
                    if i >= 2:
                        dve.wait_ge(qk_ss, per(i - 1, 10))
                    tt(sqk[:, i % 2, :], qk[i][:], qk[i][:], ALU.mult).then_inc(qk_sq, 1)
                    if i:
                        head_out(i - 1)
                head_out(9)

                items = HEADS2 * NB

                def row_max(i):
                    b = i % NB
                    dve.wait_ge(bs_s, per(i + 1, items))
                    dve.reduce_max(sm(NEGM + i % 4, 1), ps[:, 1 + i % 3, 0:(b + 1) * P], AX.X, negate=True).then_inc(bs_max, 1)

                def normed(i):
                    c, n = i % 4, P * (i % NB + 1)
                    dve.wait_ge(bs_exp, per(i + 1, items))
                    step.link(dve.reciprocal(sm(RSUM + c, 1), sm(SUM + c, 1)))
                    ts(pb[:, i % 2, 0:n], pb[:, i % 2, 0:n], sm(RSUM + c, 1), None, ALU.mult).then_inc(bs_norm, 1)

                def over_heads(row, c):
                    return tok[:, row, c * HEADS2:(c + 1) * HEADS2].unsqueeze(2).broadcast_to([P, HEADS2, 64])

                def heads_of(t):
                    return t.rearrange("p (h d) -> p h d", h=HEADS2)

                def ssd_evac(k):
                    dve.wait_ge(sd_load, per(k + 1, 11))
                    src = ps[:, 0, :]
                    if k < 4:
                        tt(heads_of(xdt[:, k, :]), heads_of(src), over_heads(0, k), ALU.mult)
                        ins = tt(heads_of(xdd[:, k, :]), heads_of(src), over_heads(4, k), ALU.mult)
                    elif k < 6:
                        ins = dve.tensor_copy(bt[:, k - 4, :, :], src.rearrange("p (c n) -> p c n", c=NB))
                    elif k < 8:
                        ins = tt(gt[:, k - 6, :, :], src.rearrange("p (c n) -> p c n", c=NB),
                                 keep.unsqueeze(1).broadcast_to([P, NB, P]), ALU.mult)
                    elif k == 8:
                        ins = dve.tensor_copy(prev[:, 0, :], src)
                    else:
                        c = k - 8
                        step.link(tt(heads_of(prev[:, c, :]), heads_of(prev[:, c - 1, :]), over_heads(3, c), ALU.mult))
                        ins = tt(prev[:, c, :], prev[:, c, :], src, ALU.add)
                    ins.then_inc(sd_evac, 1)

                def log_decay(hd):
                    dve.wait_ge(sd_e, per(hd + 1, HEADS2))
                    if hd >= 4:
                        dve.wait_ge(sd_y, per(hd - 3, HEADS2))
                    for c in range(NB):
                        w = slice(c * P, (c + 1) * P)
                        ins = ts(db[:, hd % 4, w], ps[:, SSD_BANKS[hd % 4], w], tok[:, 1, c * HEADS2 + hd:c * HEADS2 + hd + 1], 0.0,
                                 ALU.subtract, ALU.min)
                    ins.then_inc(sd_d, 1)

                row_max(0)
                row_max(1)
                normed(0)
                for i in range(items):
                    if i + 2 < items:
                        row_max(i + 2)
                    if i + 1 < items:
                        normed(i + 1)
                    if i % 2 and 3 <= i < 25:
                        ssd_evac(i // 2 - 1)
                    if i > 8 and i % 8 == 2:
                        t = i // 8 - 1
                        mix_low(t, ps[:, 6 + t % 2, :], per(8 + t + 1, 8))
                log_decay(0)
                mix_low(3, ps[:, 7, :], per(8 + 4, 8))

                def decayed(hd):
                    dve.wait_ge(sd_l, per(hd + 1, HEADS2))
                    tt(db[:, hd % 4, :], db[:, hd % 4, :], gt[:, hd // 4, :, :].rearrange("p c n -> p (c n)"), ALU.mult)
                    tt(eb[:, hd % 4, :], eb[:, hd % 4, :], xs[:, 6 + hd // 4, :], ALU.mult).then_inc(sd_m, 1)

                def gated(t):
                    dve.wait_ge(sd_y, per(2 * t + 2, HEADS2))
                    stt(yt[:, t, :], xs[:, t, :], c2("dskip", t), ps[:, 6 + t % 2, :], ALU.mult, ALU.add).then_inc(sd_yt, 1)
                    dve.wait_ge(sd_yt, per(t + 1, 4))
                    tt(yt[:, t, :], yt[:, t, :], zt[:, t, :], ALU.mult).then_inc(sd_yg, 1)

                log_decay(1)
                decayed(0)
                for hd in range(HEADS2):
                    if hd + 2 < HEADS2:
                        log_decay(hd + 2)
                    if hd + 1 < HEADS2:
                        decayed(hd + 1)
                    if hd % 2 and hd >= 3:
                        gated(hd // 2 - 1)
                gated(3)
                for t in range(4):
                    dve.wait_ge(sd_rs, per(t // 2 + 1, 2))
                    stt(yt[:, t, :], yt[:, t, :], c2("ssd", t), yrs[:, t // 2, :], ALU.mult, ALU.mult).then_inc(sd_hf, 1)
                    if t:
                        mix_low(3 + t, yt[:, t - 1, :], per(8 + 4 + t, 8))
                mix_low(7, yt[:, 3, :], per(16, 8))

                OT = UT + UP2_TILES
                for j in range(OUT2):
                    residual(j, OT + j, TL(l), 7, ((l, 4),), gate=2)
                normalize(per(3 * KT, 2 * KT), per(5, 2), lambda j: md[:, 4, j:j + 1], shift=3)

                FT2 = OT + OUT2

                def mlp(done, more, pairs, g0, gterms, inst, iterms):
                    terms = TL(l) + more

                    def hidden_low(j):
                        dve.wait_ge(g_hi, num(g0 + j + 1, gterms))
                        tt(glo[:, j, :], fv[:, j % 2, :], ghi[:, j, :].bitcast(F32), ALU.subtract).then_inc(g_lo, 1)

                    for j in range(pairs):
                        gate, up = FT2 + done + 2 * j, FT2 + done + 2 * j + 1
                        wait_evac(gate, terms)
                        dve.wait_ge(gemm_done, num(up + 1, terms))
                        if j >= 2:
                            dve.wait_ge(g_lo, num(g0 + j - 1, gterms))
                        tt(fv[:, j % 2, :], actb[:, j % 2, :], ps[:, up % 2, :], ALU.mult).then_inc(evac[up % 2], 1)
                        if j:
                            hidden_low(j - 1)
                    hidden_low(pairs - 1)
                    for j in range(KT):
                        residual(j, FT2 + done + 2 * pairs + j, terms, inst, iterms, gate=5)

                GHI = FF1_GROUPS * KT
                with dve.Fori(0, 2) as g:
                    mlp(0, ((g, 24),), 8, GHI, ((l, 22), (g, 8)), 8, ((l, 4), (g, 1)))
                mlp(48, (), 6, GHI + 16, ((l, 22),), 10, ((l, 4),))
            step.turn_ends(began, DVE_LAYER, LAYERS)

    return nc



def panels_of(np, w):
    k, n = w.shape
    out = np.zeros((n // P, P, KT, P), w.dtype)
    out[:, :, :k // P] = w.reshape(k // P, P, n // P, P).transpose(2, 1, 0, 3)
    return out.reshape(n // P, P, KT * P)


def all_panels(np, a):
    w = a["w_in"][0]
    out = [panels_of(np, np.concatenate([w[:, 1152:1280], w[:, 1408:1536], w[:, 1280:1408], w[:, 1536:1664],
                                           w[:, 2048:2432], w[:, 0:384], w[:, 1664:2048], w[:, 768:1152], w[:, 384:768]], axis=1)),
           panels_of(np, a["w_out"][0])]
    for g in range(FF1_GROUPS):
        f = slice(g * KT * P, (g + 1) * KT * P)
        out += [panels_of(np, a["w_up"][0][:, f]), panels_of(np, a["w_down"][0][f])]
    for l in range(LAYERS):
        w = a["w_in_2"][l]
        pad = np.zeros((KT * P, P - 40), w.dtype)
        out.append(panels_of(np, np.concatenate([w[:, 0:384], w[:, 384:416], w[:, 1952:1960], pad, w[:, 928:1952], w[:, 416:928]], axis=1)))
        q = a["w_q_up_2"][l].reshape(2, P, HEADS2, NOPE + ROPE)
        tiles = np.concatenate([q[..., :NOPE].reshape(2, P, 4, P), q[..., NOPE:].reshape(2, P, 2, P)], axis=2)
        up = np.zeros((4, P, 8, P), w.dtype)
        up[0:3, :, 0:4] = tiles.reshape(2, P, 3, 2, P).transpose(2, 1, 3, 0, 4).reshape(3, P, 4, P)
        kv = a["w_kv_up_2"][l].reshape(P, HEADS2, 2, 64).transpose(0, 2, 1, 3)
        up[3] = kv.reshape(P, 8, P)
        out += [up.reshape(4, P, KT * P), panels_of(np, a["w_out_2"][l])]
        w, wd, ff, f0 = a["w_gate_up_2"][l], a["w_down_2"][l], a["w_down_2"].shape[1], 0
        for pairs in FF2_PAIRS:
            f1 = f0 + pairs * P
            gate, up = panels_of(np, w[:, f0:f1]), panels_of(np, w[:, ff + f0:ff + f1])
            out += [np.stack([gate, up], axis=1).reshape(2 * pairs, P, KT * P), panels_of(np, wd[f0:f1])]
            f0 = f1
    out.append(np.zeros((RING, P, KT * P), w.dtype))
    return np.concatenate(out)


def feature_columns(np, v):
    return v.reshape(-1, P).T


def constants(np):
    c = np.zeros((P, len(CONSTS), P), np.float32)
    i = np.arange(P)
    c[:, 0] = np.eye(P)
    c[:, 1] = 1.0
    c[:, 2] = (i[:, None] // 64 == i[None] // 64) / 64.0
    c[:, 3] = (i[:, None] // 32 == i[None] // 32) / 32.0
    for m in range(P):
        if m % 32 < 16:
            c[m + 16, 4, m] = -1.0
        else:
            c[m - 16, 4, m] = 1.0
    c[:, 5] = np.where(i[None] <= i[:, None], 0.0, -1e30)
    c[:, 6] = i[None] >= i[:, None]
    return c


def attention_bias(np):
    slopes = (2.0 ** (-8.0 * np.arange(1, 7) / 6)).astype(np.float32)
    dist = np.arange(P)[:, None] + (S - P) - np.arange(S)[None]
    out = np.zeros((P, 2, 3, S), np.float32)
    for g, (window, d) in enumerate(((128, 1), (512, 4), (2048, 16))):
        open_ = (dist >= 0) & (dist <= window) & (dist % d == 0)
        for hh in range(2):
            out[:, hh, g] = np.where(open_, -slopes[2 * g + hh] * dist.astype(np.float32), np.float32(-1e30))
    return out


def kernel(**inputs):
    import numpy as np
    import concourse.bacc as bacc
    from concourse.bass_utils import run_bass_kernel_spmd

    a = {k: np.asarray(v) for k, v in inputs.items()}
    inv_freq = (1.0 / (np.float32(10000.0) ** (np.arange(0, ROPE, 2, dtype=np.float32) / np.float32(ROPE)))).astype(np.float32)
    one = np.ones((P, 1), np.float32)
    parts1 = {
        "norm1": feature_columns(np, a["norm1_g"][0]), "norm2": feature_columns(np, a["norm2_g"][0]),
        "final": feature_columns(np, a["final_g"]),
        "conv_w": a["conv_dw_w"][0].reshape(CONV_TAPS, 2, P).transpose(2, 1, 0).reshape(P, -1),
        "conv_b": feature_columns(np, a["conv_dw_b"][0]), "ln_g": feature_columns(np, a["conv_ln_g"][0]),
        "ln_b": feature_columns(np, a["conv_ln_b"][0]),
        "lru_w": a["lru_conv_w"][0].reshape(LRU_TAPS, 3, P).transpose(2, 1, 0).reshape(P, -1),
        "lru_b": feature_columns(np, a["lru_conv_b"][0]), "ba": feature_columns(np, a["lru_ba"][0]),
        "bx": feature_columns(np, a["lru_bx"][0]), "lam": feature_columns(np, a["lru_lambda"][0]),
        "c": feature_columns(np, a["c_2"][0]), "b_ada": feature_columns(np, a["b_ada_2"]),
        "invf": np.tile(inv_freq, P // len(inv_freq))[:, None], "eps6": one * np.float32(1e-6), "eps5": one * np.float32(1e-5),
    }
    cols = np.concatenate([parts1[k] for k in C1], axis=1)
    lcols = np.zeros((P, LAYERS, NC2), np.float32)
    for l in range(LAYERS):
        rows8 = np.zeros((2, P), np.float32)
        rows8[0, 32:40], rows8[1, 32:40] = a["dt_bias_2"][l], a["a_log_2"][l]
        parts2 = {
            "norm1": feature_columns(np, a["norm1_w_2"][l]), "norm2": feature_columns(np, a["norm2_w_2"][l]),
            "qa": feature_columns(np, a["q_a_norm_w_2"][l]), "kva": feature_columns(np, a["kv_a_norm_w_2"][l]),
            "qn": np.tile(a["q_nope_norm_w_2"][l], 2)[:, None], "qp": np.tile(a["q_pe_norm_w_2"][l], 4)[:, None],
            "kn": np.tile(a["k_nope_norm_w_2"][l], 2)[:, None], "kp": np.tile(a["k_pe_norm_w_2"][l], 4)[:, None],
            "conv_w": a["conv_w_2"][l].reshape(CONV2_TAPS, 8, P).transpose(2, 1, 0).reshape(P, -1),
            "conv_b": feature_columns(np, a["conv_b_2"][l]), "dt_b": rows8[0][:, None], "a_log": rows8[1][:, None],
            "dskip": np.repeat(a["d_skip_2"][l], 64).reshape(4, P).T, "ssd": feature_columns(np, a["ssd_norm_w_2"][l]),
        }
        lcols[:, l] = np.concatenate([parts2[k] for k in C2], axis=1)
    w_lru = np.zeros((P, 6, P), np.float32)
    for m, name in enumerate(("lru_wa", "lru_wx")):
        for h in range(6):
            r = slice((h % 2) * 64, (h % 2) * 64 + 64)
            w_lru[r, 3 * m + h // 2, r] = a[name][0, h]
    w_ada = a["w_ada_2"].reshape(LAYERS, KT, P, 6, KT * P).transpose(0, 3, 1, 2, 4).reshape(ADA_PAIRS * KT, P, KT * P)
    arrays = {
        "x": a["x"][0].T.reshape(KT, P, S).transpose(1, 0, 2), "cols": cols, "panels": all_panels(np, a),
        "consts": constants(np), "lcols": lcols, "w_lru": w_lru, "w_ada": w_ada, "bias": attention_bias(np),
        "positions": a["positions_2"][0],
    }
    arrays = {k: np.ascontiguousarray(v) for k, v in arrays.items()}

    nc = bacc.Bacc("TRN2", target_bir_lowering=False, num_devices=1)
    ap = {}
    for name, v in arrays.items():
        ap[name] = nc.dram_tensor(name + "_dram", v.shape, mybir.dt.from_np(v.dtype), kind="ExternalInput").ap()
    ap["out"] = nc.dram_tensor("out_dram", (P, KT, S), F32, kind="ExternalOutput").ap()
    build_program(nc, ap)
    r = run_bass_kernel_spmd(nc, [{name + "_dram": v for name, v in arrays.items()}], core_ids=[0])
    y = r.results[0]["out_dram"]
    return np.ascontiguousarray(y.transpose(1, 0, 2).reshape(KT * P, S).T[None])
```
